# Optimizing a Trainium2 kernel written in Bass

```python
import jax, jax.numpy as jnp
from jax import lax
import numpy as np
import math

D_MODEL = 1024
BATCH = 1
SEQ = 256
DEPTH = 4

N_MIXERS = 3
N_A = (DEPTH + 2) // 3
N_B = (DEPTH + 1) // 3
N_C = DEPTH // 3

N_HEADS = 16
HEAD_DIM = D_MODEL // N_HEADS
D_FF = ((8 * D_MODEL // 3 + 127) // 128) * 128
ROPE_THETA = 500000.0
ROT_DIM = HEAD_DIM // 4
Q_BLOCK = 128
EPS = 1e-6
NEG = -1e30

MOBA_BLOCK = 256
MOBA_TOPK = 3
MOBA_Q_CHUNK = 32

MLA_Q_RANK = 384
MLA_KV_RANK = 256
MLA_NOPE = 64
MLA_ROPE = 32
MLA_V = 64
MLA_IN = MLA_Q_RANK + MLA_KV_RANK + MLA_ROPE


def rms_norm(x, g):
    xf = x.astype(jnp.float32)
    y = xf * lax.rsqrt(jnp.mean(xf * xf, axis=-1, keepdims=True) + EPS)
    return (y * g.astype(jnp.float32)).astype(x.dtype)

def rotary(x, pos):
    r = x.shape[-1]
    inv = ROPE_THETA ** (-jnp.arange(0, r, 2, dtype=jnp.float32) / r)
    ang = pos.astype(jnp.float32)[:, None] * inv[None, :]
    cos, sin = jnp.cos(ang), jnp.sin(ang)
    xf = x.astype(jnp.float32)
    x1, x2 = xf[..., : r // 2], xf[..., r // 2:]
    return jnp.concatenate([x1 * cos - x2 * sin, x1 * sin + x2 * cos], axis=-1).astype(x.dtype)

def partial_rotary(x, pos):
    return jnp.concatenate([rotary(x[..., :ROT_DIM], pos), x[..., ROT_DIM:]], axis=-1)

def to_heads(t):
    b, s, _ = t.shape
    return t.reshape(b, s, N_HEADS, -1).transpose(0, 2, 1, 3)

def from_heads(t):
    b, h, s, d = t.shape
    return t.transpose(0, 2, 1, 3).reshape(b, s, h * d)

def merge_blocks(o):
    nb, b, h, q, d = o.shape
    return o.transpose(1, 2, 0, 3, 4).reshape(b, h, nb * q, d)

def swiglu(x, w_gate_up, w_down):
    g, u = jnp.split(x @ w_gate_up, 2, axis=-1)
    return (jax.nn.silu(g) * u) @ w_down

def stick_breaking_attention(x, w_qkv, w_o):
    b, s, _ = x.shape
    q, k, v = (to_heads(t) for t in jnp.split(x @ w_qkv, 3, axis=-1))
    scale = HEAD_DIM ** -0.5
    kpos = jnp.arange(s)

    def block(i):
        q0 = i * Q_BLOCK
        qb = lax.dynamic_slice_in_dim(q, q0, Q_BLOCK, axis=2)
        z = jnp.einsum('bhqd,bhkd->bhqk', qb, k).astype(jnp.float32) * scale
        qpos = q0 + jnp.arange(Q_BLOCK)
        past = kpos[None, :] < qpos[:, None]
        log_keep = jnp.where(past, -jax.nn.softplus(z), 0.0)
        tail = lax.cumsum(log_keep, axis=3, reverse=True) - log_keep
        w = jnp.where(past, jnp.exp(jax.nn.log_sigmoid(z) + tail), 0.0)
        return jnp.einsum('bhqk,bhkd->bhqd', w.astype(v.dtype), v)

    o = merge_blocks(lax.map(block, jnp.arange(s // Q_BLOCK)))
    return from_heads(o) @ w_o

def moba_attention(x, w_qkv, w_o):
    b, s, _ = x.shape
    pos = jnp.arange(s)
    q, k, v = (to_heads(t) for t in jnp.split(x @ w_qkv, 3, axis=-1))
    q, k = partial_rotary(q, pos), partial_rotary(k, pos)
    nb = -(-s // MOBA_BLOCK)
    s_pad = nb * MOBA_BLOCK
    pad = [(0, 0), (0, 0), (0, s_pad - s), (0, 0)]
    q, k, v = jnp.pad(q, pad), jnp.pad(k, pad), jnp.pad(v, pad)
    kb = k.reshape(b, N_HEADS, nb, MOBA_BLOCK, HEAD_DIM)
    vb = v.reshape(b, N_HEADS, nb, MOBA_BLOCK, HEAD_DIM)
    scale = HEAD_DIM ** -0.5

    k_mean = jnp.mean(kb.astype(jnp.float32), axis=3)
    gate = jnp.einsum('bhsd,bhnd->bhsn', q.astype(jnp.float32), k_mean)
    q_blk = jnp.arange(s_pad) // MOBA_BLOCK
    past_blk = jnp.arange(nb)[None, :] < q_blk[:, None]
    gate = jnp.where(past_blk, gate, NEG)
    topk = min(MOBA_TOPK, nb)
    _, sel = lax.top_k(gate, topk)
    sel_valid = sel < q_blk[:, None]

    bi = jnp.arange(b)[:, None, None, None]
    hi = jnp.arange(N_HEADS)[None, :, None, None]

    def chunk(c):
        q0 = c * MOBA_Q_CHUNK
        qc = lax.dynamic_slice_in_dim(q, q0, MOBA_Q_CHUNK, axis=2)
        idx = lax.dynamic_slice_in_dim(sel, q0, MOBA_Q_CHUNK, axis=2)
        valid = lax.dynamic_slice_in_dim(sel_valid, q0, MOBA_Q_CHUNK, axis=2)
        kg = kb[bi, hi, idx]
        vg = vb[bi, hi, idx]
        l_sel = jnp.einsum('bhqd,bhqjkd->bhqjk', qc, kg).astype(jnp.float32) * scale
        l_sel = jnp.where(valid[..., None], l_sel, NEG)
        l_sel = l_sel.reshape(b, N_HEADS, MOBA_Q_CHUNK, topk * MOBA_BLOCK)
        own = q0 // MOBA_BLOCK
        k_own = lax.dynamic_index_in_dim(kb, own, axis=2, keepdims=False)
        v_own = lax.dynamic_index_in_dim(vb, own, axis=2, keepdims=False)
        l_own = jnp.einsum('bhqd,bhkd->bhqk', qc, k_own).astype(jnp.float32) * scale
        cpos = q0 + jnp.arange(MOBA_Q_CHUNK)
        opos = own * MOBA_BLOCK + jnp.arange(MOBA_BLOCK)
        l_own = jnp.where(opos[None, :] <= cpos[:, None], l_own, NEG)
        p = jax.nn.softmax(jnp.concatenate([l_sel, l_own], axis=-1), axis=-1).astype(v.dtype)
        p_sel = p[..., : topk * MOBA_BLOCK].reshape(b, N_HEADS, MOBA_Q_CHUNK, topk, MOBA_BLOCK)
        p_own = p[..., topk * MOBA_BLOCK:]
        return (jnp.einsum('bhqjk,bhqjkd->bhqd', p_sel, vg)
                + jnp.einsum('bhqk,bhkd->bhqd', p_own, v_own))

    o = merge_blocks(lax.map(chunk, jnp.arange(s_pad // MOBA_Q_CHUNK)))[:, :, :s]
    return from_heads(o) @ w_o

def mla_attention(x, w_in, q_norm, w_uq, kv_norm, w_ukv, w_o):
    b, s, _ = x.shape
    pos = jnp.arange(s)
    cq, ckv, kr = jnp.split(x @ w_in, [MLA_Q_RANK, MLA_Q_RANK + MLA_KV_RANK], axis=-1)
    q = to_heads(rms_norm(cq, q_norm) @ w_uq)
    q_nope, q_rope = q[..., :MLA_NOPE], rotary(q[..., MLA_NOPE:], pos)
    kv = to_heads(rms_norm(ckv, kv_norm) @ w_ukv)
    k_nope, v = kv[..., :MLA_NOPE], kv[..., MLA_NOPE:]
    k_rope = rotary(kr, pos)
    scale = (MLA_NOPE + MLA_ROPE) ** -0.5
    kpos = jnp.arange(s)

    def block(i):
        q0 = i * Q_BLOCK
        qn = lax.dynamic_slice_in_dim(q_nope, q0, Q_BLOCK, axis=2)
        qr = lax.dynamic_slice_in_dim(q_rope, q0, Q_BLOCK, axis=2)
        logits = (jnp.einsum('bhqd,bhkd->bhqk', qn, k_nope)
                  + jnp.einsum('bhqr,bkr->bhqk', qr, k_rope)).astype(jnp.float32) * scale
        qpos = q0 + jnp.arange(Q_BLOCK)
        logits = jnp.where(kpos[None, :] <= qpos[:, None], logits, NEG)
        p = jax.nn.softmax(logits, axis=-1).astype(v.dtype)
        return jnp.einsum('bhqk,bhkd->bhqd', p, v)

    o = merge_blocks(lax.map(block, jnp.arange(s // Q_BLOCK)))
    return from_heads(o) @ w_o

def first_inputs(seed: int = 0) -> dict:
    key = jax.random.key(seed)
    ks = iter(jax.random.split(key, 32))

    def w(shape, fan_in):
        return jax.random.normal(next(ks), shape, jnp.float32) * (fan_in ** -0.5)

    def gain(shape):
        return 1.0 + 0.02 * jax.random.normal(next(ks), shape, jnp.float32)

    D = D_MODEL
    return {
        "x": jax.random.normal(next(ks), (BATCH, SEQ, D), jnp.float32),
        "norm_ffn1": gain((DEPTH, D)),
        "ffn1_w_gate_up": w((DEPTH, D, 2 * D_FF), D),
        "ffn1_w_down": w((DEPTH, D_FF, D), D_FF),
        "norm_mix": gain((DEPTH, D)),
        "norm_ffn2": gain((DEPTH, D)),
        "ffn2_w_gate_up": w((DEPTH, D, 2 * D_FF), D),
        "ffn2_w_down": w((DEPTH, D_FF, D), D_FF),
        "sb_w_qkv": w((N_A, D, 3 * D), D),
        "sb_w_o": w((N_A, D, D), D),
        "moba_w_qkv": w((N_B, D, 3 * D), D),
        "moba_w_o": w((N_B, D, D), D),
        "mla_w_in": w((N_C, D, MLA_IN), D),
        "mla_q_norm": gain((N_C, MLA_Q_RANK)),
        "mla_w_uq": w((N_C, MLA_Q_RANK, N_HEADS * (MLA_NOPE + MLA_ROPE)), MLA_Q_RANK),
        "mla_kv_norm": gain((N_C, MLA_KV_RANK)),
        "mla_w_ukv": w((N_C, MLA_KV_RANK, N_HEADS * (MLA_NOPE + MLA_V)), MLA_KV_RANK),
        "mla_w_o": w((N_C, N_HEADS * MLA_V, D), N_HEADS * MLA_V),
        "final_norm": gain((D,)),
    }

def first_block(x, norm_ffn1, ffn1_w_gate_up, ffn1_w_down, norm_mix, norm_ffn2,
              ffn2_w_gate_up, ffn2_w_down, sb_w_qkv, sb_w_o, moba_w_qkv, moba_w_o,
              mla_w_in, mla_q_norm, mla_w_uq, mla_kv_norm, mla_w_ukv, mla_w_o,
              final_norm):
    h = x
    for i in range(DEPTH):
        h = h + 0.5 * swiglu(rms_norm(h, norm_ffn1[i]), ffn1_w_gate_up[i], ffn1_w_down[i])
        hn = rms_norm(h, norm_mix[i])
        kind, j = i % N_MIXERS, i // N_MIXERS
        if kind == 0:
            mix = stick_breaking_attention(hn, sb_w_qkv[j], sb_w_o[j])
        elif kind == 1:
            mix = moba_attention(hn, moba_w_qkv[j], moba_w_o[j])
        else:
            mix = mla_attention(hn, mla_w_in[j], mla_q_norm[j], mla_w_uq[j],
                                mla_kv_norm[j], mla_w_ukv[j], mla_w_o[j])
        h = h + mix
        h = h + 0.5 * swiglu(rms_norm(h, norm_ffn2[i]), ffn2_w_gate_up[i], ffn2_w_down[i])
    return rms_norm(h, final_norm)


DEPTH_2 = 2

H_A = 4
DH_A = 64
W_A = H_A * 2 * DH_A
ROPE_THETA_2 = 10000.0
H_B = 8
N_B_2 = 64
W_B = H_B * N_B_2
R_W = 64
R_A = 64
R_G = 160
RWKV_LN_EPS = 64e-5
H_C = 4
DK_C = 128
DV_C = 128
W_C = H_C * DK_C
HGRN_CHUNK = 32
D_FF_2 = 2816
N_MOD = 9

P_A = 3 * W_A
P_B = 3 * W_B + R_W + R_A + R_G
P_C = 4 * W_C
P_G = 3 * D_MODEL
P_TOTAL = P_A + P_B + P_C + P_G


def rms_norm_2(x, w, eps=EPS):
    xf = x.astype(jnp.float32)
    y = xf * lax.rsqrt(jnp.mean(xf * xf, axis=-1, keepdims=True) + eps)
    return (y * w.astype(jnp.float32)).astype(x.dtype)

def modulate(n, shift, scale):
    return n * (1.0 + scale) + shift

def swiglu_2(u, w_gate, w_up, w_down):
    return (jax.nn.silu(u @ w_gate) * (u @ w_up)) @ w_down

def rope(t, positions):
    dh = t.shape[-1]
    inv = ROPE_THETA_2 ** (-jnp.arange(0, dh, 2, dtype=jnp.float32) / dh)
    ang = positions.astype(jnp.float32)[..., None] * inv
    cos = jnp.cos(ang)[:, :, None, None, :]
    sin = jnp.sin(ang)[:, :, None, None, :]
    tf = t.astype(jnp.float32)
    t1, t2 = tf[..., : dh // 2], tf[..., dh // 2:]
    return jnp.concatenate([t1 * cos - t2 * sin, t2 * cos + t1 * sin], axis=-1).astype(t.dtype)

def diff_attention(q, k, v, positions, qk_norm_w, lambda_qk, subln_w, layer_idx):
    B, S = q.shape[0], q.shape[1]
    q = rope(rms_norm_2(q, qk_norm_w[0]), positions)
    k = rope(rms_norm_2(k, qk_norm_w[1]), positions)
    lam_init = 0.8 - 0.6 * math.exp(-0.3 * layer_idx)
    lq = lambda_qk.astype(jnp.float32)
    lam = jnp.exp(jnp.sum(lq[0] * lq[1])) - jnp.exp(jnp.sum(lq[2] * lq[3])) + lam_init
    scale = DH_A ** -0.5
    outs = []
    for blk in range(S // Q_BLOCK):
        q0 = blk * Q_BLOCK
        kv_len = q0 + Q_BLOCK
        qb = q[:, q0:kv_len]
        kb = k[:, :kv_len]
        vb = v[:, :kv_len]
        s = jnp.einsum('bqhmd,bkhmd->bhmqk', qb, kb, preferred_element_type=jnp.float32) * scale
        causal = jnp.arange(kv_len)[None, :] <= (q0 + jnp.arange(Q_BLOCK))[:, None]
        p = jax.nn.softmax(jnp.where(causal, s, -jnp.inf), axis=-1)
        p = p[:, :, 0] - lam * p[:, :, 1]
        outs.append(jnp.einsum('bhqk,bkhe->bqhe', p.astype(v.dtype), vb))
    o = jnp.concatenate(outs, axis=1)
    o = rms_norm_2(o, subln_w) * (1.0 - lam_init)
    return o.reshape(B, S, W_A)

def token_shift(p):
    return jnp.pad(p, ((0, 0), (1, 0), (0, 0)))[:, :-1]

def rwkv7_scan(r, decay, k, v, kk, a):
    B, _, H, N = r.shape

    def step(state, inp):
        r_t, w_t, k_t, v_t, kk_t, a_t = inp
        s_kk = jnp.einsum('bhvk,bhk->bhv', state, kk_t)
        state = (state * w_t[:, :, None, :]
                 - s_kk[..., None] * (kk_t * a_t)[:, :, None, :]
                 + v_t[..., None] * k_t[:, :, None, :])
        return state, jnp.einsum('bhvk,bhk->bhv', state, r_t)

    xs = (jnp.moveaxis(t, 1, 0) for t in (r, decay, k, v, kk, a))
    _, out = lax.scan(step, jnp.zeros((B, H, N, N), jnp.float32), tuple(xs))
    return jnp.moveaxis(out, 0, 1)

def rwkv7_time_mix(p, mu, w0, w2, a0, a2, g2, k_k, k_a, r_k, ln_w, ln_b):
    B, S, _ = p.shape
    f32 = jnp.float32
    p = p + (token_shift(p) - p) * mu
    o1, o2, o3 = W_B, 2 * W_B, 3 * W_B
    r, k, v = p[..., :o1], p[..., o1:o2], p[..., o2:o3]
    xw = p[..., o3:o3 + R_W]
    xa = p[..., o3 + R_W:o3 + R_W + R_A]
    xg = p[..., o3 + R_W + R_A:]
    w = -jax.nn.softplus(-(w0 + jnp.tanh(xw) @ w2)) - 0.5
    decay = jnp.exp(-jnp.exp(w.astype(f32)))
    a = jax.nn.sigmoid(a0 + xa @ a2)
    g = jax.nn.sigmoid(xg) @ g2
    heads = lambda t: t.astype(f32).reshape(B, S, H_B, N_B_2)
    kk = heads(k * k_k)
    kk = kk / jnp.maximum(jnp.sqrt(jnp.sum(kk * kk, axis=-1, keepdims=True)), 1e-12)
    k = k * (1.0 + (a - 1.0) * k_a)
    rh, kh, vh, ah = heads(r), heads(k), heads(v), heads(a)
    o = rwkv7_scan(rh, heads(decay), kh, vh, kk, ah)
    mean = jnp.mean(o, axis=-1, keepdims=True)
    var = jnp.mean(jnp.square(o - mean), axis=-1, keepdims=True)
    o = ((o - mean) * lax.rsqrt(var + RWKV_LN_EPS)).reshape(B, S, W_B)
    o = o * ln_w.astype(f32) + ln_b.astype(f32)
    bonus = jnp.sum(rh * kh * r_k.astype(f32), axis=-1, keepdims=True) * vh
    o = o + bonus.reshape(B, S, W_B)
    return (o * g.astype(f32)).astype(p.dtype)

def hgrn2_chunked(q, k, v, log_f):
    B, S, H, dk = q.shape
    dv = v.shape[-1]
    C = HGRN_CHUNK
    n = S // C
    to_chunks = lambda t: t.reshape(B, n, C, H, t.shape[-1]).transpose(1, 0, 3, 2, 4)
    causal = jnp.tril(jnp.ones((C, C), dtype=bool))

    def step(state, inp):
        qc, kc, vc, lfc = inp
        b = jnp.cumsum(lfc, axis=2)
        o_inter = jnp.einsum('bhtk,bhkv->bhtv', qc * jnp.exp(b), state)
        diff = jnp.where(causal[:, :, None], b[:, :, :, None, :] - b[:, :, None, :, :], -jnp.inf)
        scores = jnp.einsum('bhtk,bhsk,bhtsk->bhts', qc, kc, jnp.exp(diff))
        o_intra = jnp.einsum('bhts,bhsv->bhtv', scores, vc)
        b_end = b[:, :, -1:, :]
        state = (jnp.exp(b_end[:, :, 0, :])[..., None] * state
                 + jnp.einsum('bhsk,bhsv->bhkv', kc * jnp.exp(b_end - b), vc))
        return state, o_inter + o_intra

    xs = tuple(to_chunks(t) for t in (q, k, v, log_f))
    _, o = lax.scan(step, jnp.zeros((B, H, dk, dv), jnp.float32), xs)
    return o.transpose(1, 0, 3, 2, 4).reshape(B, S, H, dv)

def hgrn2_mix(p, lower_bound, norm_w):
    B, S, _ = p.shape
    f32 = jnp.float32
    q, fz, i, g = jnp.split(p, 4, axis=-1)
    q = jax.nn.silu(q.astype(f32)).reshape(B, S, H_C, DK_C)
    lb = lower_bound.astype(f32)
    log_f = jnp.logaddexp(jnp.log(lb), jnp.log1p(-lb) + jax.nn.log_sigmoid(fz.astype(f32)))
    log_f = log_f.reshape(B, S, H_C, DK_C)
    k = -jnp.expm1(log_f)
    o = hgrn2_chunked(q, k, i.astype(f32).reshape(B, S, H_C, DV_C), log_f)
    o = rms_norm_2(o, norm_w) * jax.nn.silu(g.astype(f32).reshape(B, S, H_C, DV_C))
    return o.reshape(B, S, W_C).astype(p.dtype)

def hybrid_mixer(u, positions, layer_idx, w_in, qk_norm_w, lambda_qk, subln_w, w_out_a,
                 rwkv_mu, rwkv_w0, rwkv_w2, rwkv_a0, rwkv_a2, rwkv_g2, rwkv_k_k, rwkv_k_a,
                 rwkv_r_k, rwkv_ln_w, rwkv_ln_b, w_out_b, lower_bound, hgrn_norm_w, w_out_c, w_out):
    B, S, _ = u.shape
    p = u @ w_in
    pa = p[..., :P_A]
    pb = p[..., P_A:P_A + P_B]
    pc = p[..., P_A + P_B:P_A + P_B + P_C]
    pg = p[..., P_A + P_B + P_C:]
    qa = pa[..., :W_A].reshape(B, S, H_A, 2, DH_A)
    ka = pa[..., W_A:2 * W_A].reshape(B, S, H_A, 2, DH_A)
    va = pa[..., 2 * W_A:].reshape(B, S, H_A, 2 * DH_A)
    y_a = diff_attention(qa, ka, va, positions, qk_norm_w, lambda_qk, subln_w, layer_idx) @ w_out_a
    y_b = rwkv7_time_mix(pb, rwkv_mu, rwkv_w0, rwkv_w2, rwkv_a0, rwkv_a2, rwkv_g2,
                         rwkv_k_k, rwkv_k_a, rwkv_r_k, rwkv_ln_w, rwkv_ln_b) @ w_out_b
    y_c = hgrn2_mix(pc, lower_bound, hgrn_norm_w) @ w_out_c
    g_a, g_b, g_c = jnp.split(jax.nn.sigmoid(pg), 3, axis=-1)
    return (g_a * y_a + g_b * y_b + g_c * y_c) @ w_out

def second_inputs(seed: int = 0) -> dict:
    key = jax.random.key(seed)
    ks = iter(jax.random.split(key, 40))
    f32 = jnp.float32
    L, D = DEPTH_2, D_MODEL

    def nrm(shape, scale):
        return jax.random.normal(next(ks), shape, f32) * scale

    def gain(shape):
        return 1.0 + nrm(shape, 0.02)

    x = nrm((BATCH, SEQ, D), 1.0)
    c = nrm((BATCH, D), 1.0)
    offsets = jax.random.randint(next(ks), (BATCH, 1), 0, 4096, dtype=jnp.int32)
    positions = (offsets + jnp.arange(SEQ, dtype=jnp.int32)[None, :]).astype(jnp.int32)
    return {
        'x': x,
        'c': c,
        'positions': positions,
        'mod_w': nrm((L, D, N_MOD * D), 0.5 * D ** -0.5),
        'mod_b': nrm((L, N_MOD * D), 0.02),
        'norm_w': gain((L, 3, D)),
        'ffn_w_gate': nrm((L, 2, D, D_FF_2), D ** -0.5),
        'ffn_w_up': nrm((L, 2, D, D_FF_2), D ** -0.5),
        'ffn_w_down': nrm((L, 2, D_FF_2, D), D_FF_2 ** -0.5),
        'w_in': nrm((L, D, P_TOTAL), D ** -0.5),
        'qk_norm_w': gain((L, 2, DH_A)),
        'lambda_qk': nrm((L, 4, DH_A), 0.1),
        'subln_w': gain((L, 2 * DH_A)),
        'w_out_a': nrm((L, W_A, D), W_A ** -0.5),
        'rwkv_mu': jax.random.uniform(next(ks), (L, P_B), f32, 0.0, 1.0),
        'rwkv_w0': jax.random.uniform(next(ks), (L, W_B), f32, -6.0, 0.0),
        'rwkv_w2': nrm((L, R_W, W_B), R_W ** -0.5),
        'rwkv_a0': nrm((L, W_B), 0.1),
        'rwkv_a2': nrm((L, R_A, W_B), R_A ** -0.5),
        'rwkv_g2': nrm((L, R_G, W_B), R_G ** -0.5),
        'rwkv_k_k': 0.85 + nrm((L, W_B), 0.05),
        'rwkv_k_a': 1.0 + nrm((L, W_B), 0.05),
        'rwkv_r_k': nrm((L, H_B, N_B_2), 0.1),
        'rwkv_ln_w': gain((L, W_B)),
        'rwkv_ln_b': nrm((L, W_B), 0.02),
        'w_out_b': nrm((L, W_B, D), W_B ** -0.5),
        'hgrn_lower_bounds': nrm((L, W_C), 0.5),
        'hgrn_norm_w': gain((L, DV_C)),
        'w_out_c': nrm((L, W_C, D), W_C ** -0.5),
        'w_out': nrm((L, D, D), D ** -0.5),
    }

def second_block(x, c, positions, mod_w, mod_b, norm_w, ffn_w_gate, ffn_w_up, ffn_w_down,
              w_in, qk_norm_w, lambda_qk, subln_w, w_out_a,
              rwkv_mu, rwkv_w0, rwkv_w2, rwkv_a0, rwkv_a2, rwkv_g2, rwkv_k_k, rwkv_k_a,
              rwkv_r_k, rwkv_ln_w, rwkv_ln_b, w_out_b,
              hgrn_lower_bounds, hgrn_norm_w, w_out_c, w_out):
    B, S, D = x.shape
    lb = jnp.cumsum(jax.nn.softmax(hgrn_lower_bounds.astype(jnp.float32), axis=0), axis=0)
    lb = lb - lb[0]
    cond = jax.nn.silu(c)
    h = x
    for l in range(DEPTH_2):
        mod = (cond @ mod_w[l] + mod_b[l]).reshape(B, N_MOD, D)
        m = [mod[:, j, None, :] for j in range(N_MOD)]
        u = modulate(rms_norm_2(h, norm_w[l, 0]), m[0], m[1])
        h = h + 0.5 * m[2] * swiglu_2(u, ffn_w_gate[l, 0], ffn_w_up[l, 0], ffn_w_down[l, 0])
        u = modulate(rms_norm_2(h, norm_w[l, 1]), m[3], m[4])
        y = hybrid_mixer(u, positions, l, w_in[l], qk_norm_w[l], lambda_qk[l], subln_w[l], w_out_a[l],
                         rwkv_mu[l], rwkv_w0[l], rwkv_w2[l], rwkv_a0[l], rwkv_a2[l], rwkv_g2[l],
                         rwkv_k_k[l], rwkv_k_a[l], rwkv_r_k[l], rwkv_ln_w[l], rwkv_ln_b[l], w_out_b[l],
                         lb[l], hgrn_norm_w[l], w_out_c[l], w_out[l])
        h = h + m[5] * y
        u = modulate(rms_norm_2(h, norm_w[l, 2]), m[6], m[7])
        h = h + 0.5 * m[8] * swiglu_2(u, ffn_w_gate[l, 1], ffn_w_up[l, 1], ffn_w_down[l, 1])
    return h


def setup_inputs(seed=0):
    out = dict(first_inputs(seed))
    for name, value in second_inputs(seed + 1).items():
        if name != "x":
            out[name + "_2"] = value
    return out


def reference(
    x, norm_ffn1, ffn1_w_gate_up, ffn1_w_down, norm_mix, norm_ffn2, ffn2_w_gate_up, ffn2_w_down,
    sb_w_qkv, sb_w_o, moba_w_qkv, moba_w_o, mla_w_in, mla_q_norm, mla_w_uq, mla_kv_norm,
    mla_w_ukv, mla_w_o, final_norm, c_2, positions_2, mod_w_2, mod_b_2, norm_w_2, ffn_w_gate_2,
    ffn_w_up_2, ffn_w_down_2, w_in_2, qk_norm_w_2, lambda_qk_2, subln_w_2, w_out_a_2, rwkv_mu_2,
    rwkv_w0_2, rwkv_w2_2, rwkv_a0_2, rwkv_a2_2, rwkv_g2_2, rwkv_k_k_2, rwkv_k_a_2, rwkv_r_k_2,
    rwkv_ln_w_2, rwkv_ln_b_2, w_out_b_2, hgrn_lower_bounds_2, hgrn_norm_w_2, w_out_c_2, w_out_2,
):
    x = first_block(
        x, norm_ffn1, ffn1_w_gate_up, ffn1_w_down, norm_mix, norm_ffn2, ffn2_w_gate_up,
        ffn2_w_down, sb_w_qkv, sb_w_o, moba_w_qkv, moba_w_o, mla_w_in, mla_q_norm, mla_w_uq,
        mla_kv_norm, mla_w_ukv, mla_w_o, final_norm,
    )
    return second_block(
        x, c_2, positions_2, mod_w_2, mod_b_2, norm_w_2, ffn_w_gate_2, ffn_w_up_2, ffn_w_down_2,
        w_in_2, qk_norm_w_2, lambda_qk_2, subln_w_2, w_out_a_2, rwkv_mu_2, rwkv_w0_2, rwkv_w2_2,
        rwkv_a0_2, rwkv_a2_2, rwkv_g2_2, rwkv_k_k_2, rwkv_k_a_2, rwkv_r_k_2, rwkv_ln_w_2,
        rwkv_ln_b_2, w_out_b_2, hgrn_lower_bounds_2, hgrn_norm_w_2, w_out_c_2, w_out_2,
    )


_drawn_inputs = setup_inputs


def setup_inputs(seed=0):
    import zlib

    import numpy as np

    out = dict(_drawn_inputs(seed))
    spreads = {}
    factors = {'norm_ffn1': 3.247,
     'norm_ffn2': 3.848,
     'mla_q_norm': 8.0,
     'mla_kv_norm': 8.0,
     'final_norm': 2.759,
     'norm_w_2': 6.021,
     'qk_norm_w_2': 22.105,
     'lambda_qk_2': 5.908,
     'subln_w_2': 200.0,
     'rwkv_w2_2': 4.087,
     'rwkv_a0_2': 8.0,
     'rwkv_k_k_2': 200.0,
     'rwkv_k_a_2': 4.399,
     'rwkv_ln_w_2': 200.0,
     'rwkv_ln_b_2': 200.0,
     'hgrn_lower_bounds_2': 8.0,
     'hgrn_norm_w_2': 37.126}
    for name, (base, spread) in spreads.items():
        noise = np.random.default_rng([zlib.crc32(name.encode()), seed]).standard_normal(out[name].shape)
        drawn = base * np.exp(spread * noise) if base else spread * noise
        out[name] = __import__('jax').numpy.asarray(drawn.astype(out[name].dtype))
    for name, factor in factors.items():
        out[name] = (out[name] * factor).astype(out[name].dtype)
    return out
```

```python
import math
from contextlib import ExitStack

import numpy as np

import concourse.bass as bass
from concourse import mybir

F32 = mybir.dt.float32
F32R = mybir.dt.float32r
I32 = mybir.dt.int32
ALU = mybir.AluOpType
ACT = mybir.ActivationFunctionType
AX = mybir.AxisListType

P = 128
D = 1024
KC = D // P
SEQ = 256
NT = SEQ // P
DEPTH = 4
DEPTH_2 = 2
EPS = 1e-6
NEG = -1e30
D_FF = 2816
FFB = 256
FF_STEPS = D_FF // FFB
N_HEADS = 16
DH = 64
N_PAIRS = N_HEADS // 2
ROT_DIM = DH // 4
MLA_Q_RANK, MLA_KV_RANK, MLA_ROPE, MLA_NOPE, MLA_V = 384, 256, 32, 64, 64
MLA_IN = MLA_Q_RANK + MLA_KV_RANK + MLA_ROPE
MLA_QH = MLA_NOPE + MLA_ROPE
ROPE_THETA = 500000.0
ROPE_THETA_2 = 10000.0

N_MOD = 9
H_A, DH_A = 4, 64
W_A = H_A * 2 * DH_A
H_B, N_B = 8, 64
W_B = H_B * N_B
R_W, R_A, R_G = 64, 64, 160
RWKV_LN_EPS = 64e-5
H_C, DK_C = 4, 128
W_C = H_C * DK_C
P_A = 3 * W_A
P_B = 3 * W_B + R_W + R_A + R_G
P_C = 4 * W_C
BC = W_B // P
BLK = 64
LEVELS = [1, 2, 4, 8, 16, 32, 64]

VEC_1 = {"gains": 0, "q_norm": 12 * KC, "kv_norm": 12 * KC + 3, "c": 12 * KC + 5, "index": 13 * KC + 5}
VEC_1_ROWS = 13 * KC + 5 + NT
VEC_2 = {}
_row = 0
for _name, _rows in (("mu", 15), ("w0", BC), ("a0", BC), ("k_k", BC), ("k_a", BC), ("r_k", BC), ("ln_w", BC),
                     ("ln_b", BC), ("subln", 1), ("hnorm", 1), ("bound0", BC), ("bound1", BC),
                     ("norm_w", 3 * KC)):
    VEC_2[_name] = _row
    _row += _rows
VEC_2_ROWS = _row
MOD_ROWS = N_MOD * KC
VEC_ROWS = [VEC_1_ROWS, VEC_2_ROWS, VEC_2_ROWS, MOD_ROWS, MOD_ROWS]

DMA = 16


def rounded(ap):
    return ap.bitcast(F32R)


class Step:

    def __init__(self, s, j=None):
        self.s, self.j = s, j

    def n(self, per=1, add=0):
        fixed = per * self.s + add
        return fixed if self.j is None else fixed + self.j * (2 * per)

    def half(self, per, add=0):
        fixed = per * (self.s // 2) + add
        return fixed if self.j is None else fixed + self.j * per

    def plus(self, k):
        return Step(self.s + k, self.j)

    @property
    def odd(self):
        return self.s % 2


class Events:

    def __init__(self, sem, *names):
        self.sem, self.first, self.order = sem, {}, []
        for name, times in names:
            self.first[name] = len(self.order) + 1
            self.order += [name] * times
        self.raised = 0

    def at(self, layer, name, k=0):
        return self.sem, layer * len(self.order) + self.first[name] + k

    def next(self, name):
        assert self.order[self.raised % len(self.order)] == name, (name, self.raised)
        self.raised += 1
        return self.sem, 1


class Counts:

    def __init__(self):
        self.load = 0
        self.ffn = 0
        self.even = 0
        self.odd = 0
        self.norm = 0
        self.hidden = 0
        self.pair = 0
        self.sb = 0
        self.lin = 0
        self.sq = 0
        self.rstd = 0
        self.small = 0
        self.ffns = 0
        self.shift = 0
        self.diff = 0
        self.scaled = 0
        self.landed = [0, 0]
        self.first = 0

    def dmas(self, w, per):
        first = self.first + (self.first + w.s) % 2
        fixed = DMA * (self.landed[w.odd] + per * ((w.s - first) // 2 + 1))
        return fixed if w.j is None else fixed + w.j * (DMA * per)

    def loaded(self, loads, per):
        for w in range(self.first, self.first + loads):
            self.landed[w % 2] += per
        self.load = self.first = self.first + loads


def run_steps(engine, total, head, tail, step):
    for k in range(head):
        step(k, None)
    if total > head + tail:
        with engine.Fori(0, (total - head - tail) // 2) as j:
            for k in (head, head + 1):
                step(k, j)
    for k in range(total - tail, total):
        step(k, None)


def program(nc, A, out):
    ctx = ExitStack()
    with ctx:
        def sb(name, shape, dt=F32):
            return ctx.enter_context(nc.sbuf_tensor(name, shape, dt))

        def sem(name):
            return ctx.enter_context(nc.semaphore(name))

        bank = [ctx.enter_context(nc.psum_tensor(f"bank{i}", [P, 512], F32)) for i in range(8)]
        proj_ps = bank[0:2]
        turn_ps = bank[2]
        down_ps = bank[3:7]
        aux_ps = bank[7]

        whole = ExitStack()

        def sb_whole(name, shape):
            return whole.enter_context(nc.sbuf_tensor(name, shape, F32))

        wproj = [sb_whole(f"wproj{i}", [P, KC * 512]) for i in range(2)]
        wdown = [sb_whole(f"wdown{i}", [P, 2, D]) for i in range(2)]
        xT = sb_whole("xT", [P, KC, SEQ])
        oT = [sb_whole(f"oT{i}", [P, BC, SEQ]) for i in range(2)]
        arena = sb_whole("arena", [P, ARENA])
        whole.close()
        wproj_lo = [sb(f"wproj_lo{i}", [P, KC * 512]) for i in range(2)]
        wdown_lo = [sb(f"wdown_lo{i}", [P, 2, D]) for i in range(2)]
        x_lo = sb("x_lo", [P, KC, SEQ])
        x_hi_parts = [sb(f"x_hi{i}", [P, BC, SEQ]) for i in range(2)]
        sb("under_gate_and_act", [P, 2 * NT * FFB])
        actT_lo = [sb(f"actT_lo{i}", [P, 512]) for i in range(2)]
        wdown_hi = [sb(f"wdown_hi{i}", [P, 2, D]) for i in range(2)]
        actT_hi = [sb(f"actT_hi{i}", [P, 512]) for i in range(2)]
        used = 2 * NT * FFB + 2 * 512 + 2 * 2 * D + 2 * 512
        sb("under_constants", [P, CONSTANTS_END - used])
        wproj_hi = [sb(f"wproj_hi{i}", [P, KC * 512]) for i in range(2)]
        sb("under_rest", [P, ARENA - CONSTANTS_END - 2 * KC * 512])
        hid = sb("hid", [P, NT, D])
        place = [0]

        def view(*shape):
            size = int(np.prod(shape))
            at, place[0] = place[0], place[0] + size
            assert place[0] <= ARENA, place[0]
            flat = arena[:, at:at + size]
            names = "abcd"[:len(shape)]
            return flat if len(shape) == 1 else flat.rearrange(
                f"p ({' '.join(names)}) -> p {' '.join(names)}", **dict(zip(names, shape)))

        tok = sb("tok", [P, NT, D])
        ident = sb("ident", [P, P])
        causal = sb("causal", [P, NT, SEQ])
        ones = sb("ones", [P, SEQ])
        vec = sb("vec", [P, 5, P])
        gains = vec[:, 0, 0:96].rearrange("p (n c) -> p n c", c=KC)
        mla_gains = vec[:, 0, 96:101]
        sumsq = sb("sumsq", [P, 4])
        rstd = sb("rstd", [P, 4])
        minus_half = sb("minus_half", [P, 16])
        gate_sb = view(NT, FFB)
        act_sb = view(NT, FFB)
        actT = [view(512) for i in range(2)]
        constants_at = place[0] + 2 * 2 * D + 2 * 512
        place[0] = 0
        NROPE = ROT_DIM // 2 + MLA_ROPE // 2 + DH // 2
        freq = sb("freq", [P, NROPE])
        pos_i = sb("pos_i", [P, NT], I32)
        pos = sb("pos", [P, 2, NT])
        ang = sb("ang", [P, 2, NT, NROPE])
        angk = sb("angk", [P, 2, NT, NROPE])
        trig = sb("trig", [P, 2, NT, NROPE])
        cos_t, sin_t = trig[:, 0], trig[:, 1]
        qkv = [view(NT, 448) for i in range(2)]
        cat = view(NT, 4, MLA_QH)
        qkT = view(2, 512)
        score = view(2, NT, SEQ)
        soft = view(2, NT, SEQ)
        negmax = sb("negmax", [P, 2, NT])
        rowsum = sb("rowsum", [P, 2, NT])
        rinv = sb("rinv", [P, 2, NT])
        probT = view(2, 384)
        rt = view(4, NT * 4 * 32)
        qkw = sb("qkw", [P, DEPTH_2, 2, DH_A])
        lqk = view(DEPTH_2, 4, DH_A)
        lam = sb("lam", [P, DEPTH_2])
        lam_e = sb("lam_e", [P, DEPTH_2, 2])
        heads_ss = sb("heads_ss", [P, 8])
        heads_rs = sb("heads_rs", [P, 8])
        ln_ss = sb("ln_ss", [P, 16])
        ln_rs = sb("ln_rs", [P, 16])
        o_head = soft.rearrange("p h t k -> p (h t k)")[:, 0:3 * SEQ].rearrange(
            "p (m t d) -> p m t d", m=3, t=NT)
        condT = view(KC, P)
        cond = sb("cond", [P, KC])
        modrow = sb("modrow", [P, 3, D])
        modcol = sb("modcol", [P, MOD_ROWS])
        modA = sb("modA", [P, 3, KC])
        oT.append(sb("oT2", [P, BC, SEQ]))


        def x_hi(c):
            return x_hi_parts[c // BC][:, c % BC, :]

        gate = sb("gate", [P, NT, 512])
        lora_w = sb("lora_w", [P, 3, W_B])
        lvl = sb("lvl", [P, len(LEVELS), P])
        prod_mask = sb("prod_mask", [P, 2, 2, P])
        headsum = sb("headsum", [P, P])
        restart = sb("restart", [P, SEQ])
        one_less = sb("one_less", [P, 19])
        lows = sb("lows", [P, 6, BC])
        past01 = view(NT, SEQ)
        pastneg = view(NT, SEQ)
        grow = view(D)
        kr_sb = view(NT, MLA_ROPE)
        vec_row = view(5, P)
        assert place[0] <= CONSTANTS_END and constants_at <= place[0]
        place[0] = 0
        rw_r, rw_k, rw_v_, rw_a = (view(BC, SEQ) for _ in range(4))
        rw_kk, rw_p, rw_t0, rw_t1, rw_t2 = (view(BC, SEQ) for _ in range(5))
        rw_xwa, rw_xg1, rw_xg2 = view(SEQ), view(SEQ), view(SEQ)
        kr_all = view(BC, 2, SEQ)
        kh, bh = view(BC, SEQ), view(BC, SEQ)
        k1, b1 = view(BC, SEQ), view(BC, SEQ)
        kr_in = view(BC, 2, P)
        k_end, b_end = view(BC, P), view(BC, P)
        v_tok = view(NT, W_B)
        w_tok, u_neg = view(W_B), view(W_B)
        assert place[0] <= ARENA
        place[0] = 0
        mats = view(8, 4, P)
        inv, invT, y_sb, part = (view(8, P) for _ in range(4))
        kb_tok = view(2, W_B)
        state = view(BC, P)
        place[0] = 0
        hq, hk, hf, hs = (view(BC, SEQ) for _ in range(4))
        h_t, h_e = view(BC, SEQ), view(BC, SEQ)
        h_x = [view(BC, SEQ) for _ in range(2)]
        h_acc = view(8, P)
        h_cross = view(4, P)
        h_v, h_g = view(NT, W_C), view(NT, W_C)
        mla_c = view(NT, MLA_IN)

        const_in = sem("const_in")
        x_in = sem("x_in")
        w_in = [sem("wproj_in0"), sem("wproj_in1")]
        proj_done = sem("proj_done")
        d_in = [sem("wdown_in0"), sem("wdown_in1")]
        f_in = [sem("ffn_in0"), sem("ffn_in1")]
        cols_hi, cols_lo = sem("cols_hi"), sem("cols_lo")
        rows_rounded, rows_lo = sem("rows_hi"), sem("rows_lo")
        x_split, act_split = sem("x_split"), sem("act_split")
        ff_silu, ff_act = sem("ff_silu"), sem("ff_act")
        ff_turn, ff_copied, ff_down = sem("ff_turn"), sem("ff_copied"), sem("ff_down")
        nm_sq, nm_scaled = sem("nm_sq"), sem("nm_scaled")
        rstd_ready = sem("rstd_ready")
        tr_even, tr_odd = sem("tr_even"), sem("tr_odd")
        ev_even, ev_odd = sem("ev_even"), sem("ev_odd")
        hid_ready = sem("hid_ready")
        masks_ready = sem("masks_ready")
        trig_ang, trig_ready = sem("trig_ang"), sem("trig_ready")
        at_ev, at_prep = sem("at_ev"), sem("at_prep")
        at_turn, at_turned = sem("at_turn"), sem("at_turned")
        at_s, at_l, at_e = sem("at_s"), sem("at_l"), sem("at_e")
        sb_soft, sb_arg = sem("sb_soft"), sem("sb_arg")
        at_pt, at_ptc, at_pv, at_o = sem("at_pt"), sem("at_ptc"), sem("at_pv"), sem("at_o")
        ln_ev = sem("ln_ev")
        out_done = sem("out_done")
        vec_in, vec_turned, vec_ready = sem("vec_in"), sem("vec_turned"), sem("vec_ready")
        lam_terms, lam_exp = sem("lam_terms"), sem("lam_exp")
        cond_ready, condT_ready = sem("cond_ready"), sem("condT_ready")
        head_ss, head_rs = sem("head_ss"), sem("head_rs")
        small_in = sem("small_in")
        shift_part = sem("shift_part")
        tiles = range(NT)
        LV = len(LEVELS) - 1
        rw_v = Events(sem("rwkv_vector"), ("kk_sq", 1), ("rk", 1), ("expo", 1), ("scaled", 1),
                      ("mats0", 8), ("xt0", 1), ("x0", 1 + LV), ("un0", 1), ("state_c", 1),
                      ("mats1", 8), ("xt1", 1), ("x1", 1 + LV), ("un1", 1),
                      ("ln_ss", 1), ("ln", 1), ("out", 1))
        rw_pe = Events(sem("rwkv_tensor"), ("lora", 1), ("kk_ss", 1), ("vtok", 1), ("bonus", 1), ("kb_turn", 1),
                       ("mat0", 8), ("x00", 1), *[(f"yz0_{i}", 2) for i in range(LV)],
                       ("w0", 1), ("u0", 1), ("o0", 1), ("state", 1),
                       ("mat1", 8), ("x01", 1), *[(f"yz1_{i}", 2) for i in range(LV)],
                       ("w1", 1), ("u1", 1), ("o1", 1))
        rw_act = Events(sem("rwkv_scalar"), ("lora_in", 1), ("lora_out", 1), ("kk_norm", 1), ("vtok_c", 1),
                        ("exps", 1), ("kb_c", 1), ("yc0", LV), ("wc0", 1), ("oc0", 1),
                        ("yc1", LV), ("wc1", 1), ("oc1", 1))
        rw_pool = Events(sem("rwkv_pool"), ("et0", LV), ("et1", LV), ("ln_rs", 1))
        n_lv = len(LEVELS) + 1
        hg_abs, hg_ln = Events(sem("hgrn_abs"), ("abs", 1)), Events(sem("hgrn_ln"), ("ln", 1))
        hb_abs, hb_ln = Events(sem("hgrn_abs_lb"), ("abs", 1)), Events(sem("hgrn_ln_lb"), ("ln", 1))
        hg_ex = Events(sem("hgrn_exp"), ("ex", n_lv))
        hg_x = Events(sem("hgrn_x"), ("x", n_lv))
        hg_upd = Events(sem("hgrn_upd"), ("upd", n_lv))
        hg_acc = Events(sem("hgrn_acc"), ("acc", n_lv + 1))
        hg_s = Events(sem("hgrn_s"), ("s", n_lv + 1))
        hg_o = Events(sem("hgrn_o"), ("o", 1))
        hg_oc = Events(sem("hgrn_oc"), ("oc", 1))
        hg_ss, hg_rs = Events(sem("hgrn_ss"), ("ss", 1)), Events(sem("hgrn_rs"), ("rs", 1))
        hg_out = Events(sem("hgrn_out"), ("out", 1))
        low_d, low_s = sem("low_d"), sem("low_s")
        y_ready = sem("y_ready")

        def halves(x, m):
            return x.rearrange("p c s -> p (c s)").rearrange("p (g h j) -> p g h j", h=2, j=m)

        def shift_places(b, half):
            if b < 3:
                dst = (rw_r, rw_k, rw_v_)[b]
                return [(q, dst[:, 2 * half + q]) for q in range(2)]
            return [(0, rw_xwa), (1, rw_xg1)] if half == 0 else [(0, rw_xg2)]

        block = ctx.enter_context(nc.Block())

        @block.gpsimd
        def _(pool):
            nc.gpsimd.memset(ident[:, :], 0.0)
            nc.gpsimd.memset(causal[:], 0.0)
            nc.gpsimd.memset(past01[:], 1.0)
            nc.gpsimd.memset(pastneg[:], 0.0)
            nc.gpsimd.memset(ones[:, :], 1.0)
            nc.gpsimd.memset(minus_half[:, :], -0.5)
            nc.gpsimd.memset(vec_row[:], 0.0)
            for filled in (headsum, restart, prod_mask, lvl):
                nc.gpsimd.memset(filled[:], 1.0)
            pool.drain()
            nc.gpsimd.affine_select(out=headsum[:].rearrange("p (a b) -> p a b", a=2)[0:64],
                                    in_=headsum[:].rearrange("p (a b) -> p a b", a=2)[0:64],
                                    compare_op=ALU.is_ge, fill=0.0, base=0, pattern=[[-1, 2], [0, 64]],
                                    channel_multiplier=0)
            nc.gpsimd.affine_select(out=headsum[:].rearrange("p (a b) -> p a b", a=2)[64:128],
                                    in_=headsum[:].rearrange("p (a b) -> p a b", a=2)[64:128],
                                    compare_op=ALU.is_ge, fill=0.0, base=-1, pattern=[[1, 2], [0, 64]],
                                    channel_multiplier=0)
            pool.drain()
            nc.gpsimd.affine_select(out=restart[:].rearrange("p (a b) -> p a b", b=BLK),
                                    in_=restart[:].rearrange("p (a b) -> p a b", b=BLK), compare_op=ALU.is_gt,
                                    fill=0.0, base=0, pattern=[[0, SEQ // BLK], [1, BLK]], channel_multiplier=0)
            for kb in range(2):
                for kind in range(2):
                    m = prod_mask[:, kb, kind, :]
                    nc.gpsimd.affine_select(out=m, in_=m, compare_op=ALU.is_ge, fill=0.0, base=kind - 1,
                                            pattern=[[1, P]], channel_multiplier=-1)
            for i, m in enumerate(LEVELS):
                nb = P // (2 * m)
                both = lvl[:, i, :].rearrange("p (g h j) -> p g h j", g=nb, h=2)
                nc.gpsimd.memset(both[:, :, 0, :], 0.0)
                half = both[:, :, 1, :]
                nc.gpsimd.affine_select(out=half, in_=half, compare_op=ALU.is_ge, fill=0.0, base=0,
                                        pattern=[[-2 * m, nb], [0, m]], channel_multiplier=1)
                pool.drain()
                nc.gpsimd.affine_select(out=half, in_=half, compare_op=ALU.is_ge, fill=0.0, base=m - 1,
                                        pattern=[[2 * m, nb], [0, m]], channel_multiplier=-1)
            nc.gpsimd.affine_select(out=ident[:, :], in_=ident[:, :], compare_op=ALU.not_equal, fill=1.0,
                                    base=0, pattern=[[-1, P]], channel_multiplier=1)
            nc.gpsimd.affine_select(out=causal[:], in_=causal[:], compare_op=ALU.is_ge, fill=NEG,
                                    base=0, pattern=[[P, NT], [-1, SEQ]], channel_multiplier=1)
            nc.gpsimd.affine_select(out=past01[:], in_=past01[:], compare_op=ALU.is_ge, fill=0.0,
                                    base=-1, pattern=[[P, NT], [-1, SEQ]], channel_multiplier=1)
            nc.gpsimd.affine_select(out=pastneg[:], in_=pastneg[:], compare_op=ALU.is_ge, fill=NEG,
                                    base=-1, pattern=[[P, NT], [-1, SEQ]],
                                    channel_multiplier=1).then_inc(masks_ready, 1)
            n = Counts()

            def inverse_rms(*parts):
                n.sq += 2
                pool.wait_ge(nm_sq, n.sq)
                for a, b, width in parts:
                    nc.gpsimd.tensor_scalar(rstd[:, a:b], sumsq[:, a:b], 1.0 / width, EPS, ALU.mult, ALU.add)
                pool.drain()
                nc.gpsimd.tensor_tensor(rstd[:, 0:b], rstd[:, 0:b], minus_half[:, 0:b], ALU.pow).then_inc(rstd_ready, 1)

            for l in range(DEPTH):
                inverse_rms((0, 2, D))
                inverse_rms((0, 2, D))
                if l % 3 == 2:
                    inverse_rms((0, 2, MLA_Q_RANK), (2, 4, MLA_KV_RANK))
                inverse_rms((0, 2, D))

            def heads_rms(columns, width, eps):
                pool.wait_ge(head_ss, n.diff + 1)
                nc.gpsimd.tensor_scalar(heads_rs[:, 0:columns], heads_ss[:, 0:columns], 1.0 / width, eps,
                                        ALU.mult, ALU.add)
                pool.drain()
                nc.gpsimd.tensor_tensor(heads_rs[:, 0:columns], heads_rs[:, 0:columns],
                                        minus_half[:, 0:columns], ALU.pow).then_inc(head_rs, 1)
                n.diff += 1

            def power(width, eps):
                nc.gpsimd.tensor_scalar(ln_rs[:], ln_ss[:], 1.0 / width, eps, ALU.mult, ALU.add)
                pool.drain()
                return nc.gpsimd.tensor_tensor(ln_rs[:], ln_rs[:], minus_half[:], ALU.pow)

            inverse_rms((0, 2, D))
            for l in range(DEPTH_2):
                inverse_rms((0, 2, D))
                inverse_rms((0, 2, D))
                heads_rms(8, DH_A, EPS)
                for h in range(H_A):
                    if h < H_A - 1:
                        heads_rms(8, DH_A, EPS)
                    heads_rms(2, 2 * DH_A, EPS)
                for t in range(NT):
                    pool.wait_ge(*rw_v.at(l, f"mats{t}", 7))
                    for i in range(LV):
                        if i:
                            pool.wait_ge(*rw_pe.at(l, f"yz{t}_{i - 1}"))
                        nc.gpsimd.tensor_tensor(part[:], mats[:, :, 2, :],
                                                lvl[:, i + 1, :].unsqueeze(1).broadcast_to([P, 8, P]),
                                                ALU.mult).then_inc(*rw_pool.next(f"et{t}"))
                pool.wait_ge(*rw_v.at(l, "ln_ss"))
                power(N_B, RWKV_LN_EPS).then_inc(*rw_pool.next("ln_rs"))
                pool.wait_ge(*hg_ss.at(l, "ss"))
                power(DK_C, EPS).then_inc(*hg_rs.next("rs"))
                inverse_rms((0, 2, D))

        @block.sync
        def _(sp):
            n = Counts()

            def room(st):
                if st.s >= 2:
                    sp.wait_ge(proj_done, st.n(2, -2))

            def ffn(gate, up, down):
                def columns(f, w, d):
                    room(w)
                    dst = wproj[w.odd][:, :].rearrange("p (c n) -> p c n", c=KC)
                    for half, src in enumerate((gate, up)):
                        sp.dma_start(dst[:, :, half * FFB:(half + 1) * FFB],
                                     src.rearrange("(c p) n -> p c n", p=P)[:, :, bass.ds(f.n(FFB), FFB)]
                                     ).then_inc(f_in[d.odd], DMA)

                def rows(f, d):
                    if d.s >= 2:
                        sp.wait_ge(ff_down, d.n(1, -1))
                    sp.dma_start(wdown[d.odd][:], down.rearrange("(f c p) n -> f p c n", p=P, c=2)[
                        bass.ds(f.n(), 1)].rearrange("f p c n -> (f p) c n")).then_inc(d_in[d.odd], DMA)

                columns(Step(0), Step(n.load), Step(n.ffn))

                def load(f, w, d):
                    columns(f.plus(1), w.plus(1), d.plus(1))
                    rows(f, d)
                run_steps(sp, FF_STEPS - 1, 2, 0, lambda k, j:
                          load(Step(k, j), Step(n.load + k, j), Step(n.ffn + k, j)))
                rows(Step(FF_STEPS - 1), Step(n.ffn + FF_STEPS - 1))
                n.load += FF_STEPS
                n.ffn += FF_STEPS

            def heads(w_qkv, pairs=N_PAIRS):
                def load(i, w):
                    room(w)
                    dst = wproj[w.odd][:, 0:KC * 384].rearrange("p (c s n) -> p c s n", c=KC, s=3)
                    src = w_qkv.rearrange("(c p) (s n) -> p c s n", p=P, s=3)
                    for s in range(3):
                        sp.dma_start(dst[:, :, s], src[:, :, s, bass.ds(i.n(P), P)]).then_inc(w_in[w.odd], DMA)
                run_steps(sp, pairs, 0, 0, lambda k, j: load(Step(k, j), Step(n.load + k, j)))
                n.load += pairs

            def heads_mla(w_uq, w_ukv):
                def load(i, w):
                    room(w)
                    buf = wproj[w.odd]
                    sp.dma_start(buf[:, 0:576].rearrange("p (c n) -> p c n", c=3),
                                 w_uq.rearrange("(c p) n -> p c n", p=P)[:, :, bass.ds(i.n(192), 192)]
                                 ).then_inc(w_in[w.odd], DMA)
                    sp.dma_start(buf[:, 576:1088].rearrange("p (c n) -> p c n", c=2),
                                 w_ukv.rearrange("(c p) n -> p c n", p=P)[:, :, bass.ds(i.n(256), 256)]
                                 ).then_inc(w_in[w.odd], DMA)
                run_steps(sp, N_PAIRS, 0, 0, lambda k, j: load(Step(k, j), Step(n.load + k, j)))
                n.load += N_PAIRS

            def linear(w, blocks):
                kc = w.shape[0] // P
                for lo, width in blocks:
                    st = Step(n.load)
                    room(st)
                    dst = wproj[st.odd][:, 0:kc * width].rearrange("p (c n) -> p c n", c=kc)
                    src = w.rearrange("(c p) n -> p c n", p=P)
                    mid = kc // 2
                    for a, b in ((0, mid), (mid, kc)):
                        sp.dma_start(dst[:, a:b], src[:, a:b, lo:lo + width]).then_inc(w_in[st.odd], DMA)
                    n.load += 1

            sp.dma_start(hid[:], A["x"].rearrange("b (t p) d -> p (b t) d", p=P)).then_inc(x_in, DMA)
            for l in range(DEPTH):
                ffn(A["ffn1_w_gate_up"][l, :, 0:D_FF], A["ffn1_w_gate_up"][l, :, D_FF:], A["ffn1_w_down"][l])
                if l % 3 == 0:
                    heads(A["sb_w_qkv"][l // 3])
                    linear(A["sb_w_o"][l // 3], WO_BLOCKS)
                elif l % 3 == 1:
                    heads(A["moba_w_qkv"][l // 3])
                    linear(A["moba_w_o"][l // 3], WO_BLOCKS)
                else:
                    linear(A["mla_w_in"][l // 3], MLA_BLOCKS)
                    heads_mla(A["mla_w_uq"][l // 3], A["mla_w_ukv"][l // 3])
                    linear(A["mla_w_o"][l // 3], WO_BLOCKS)
                ffn(A["ffn2_w_gate_up"][l, :, 0:D_FF], A["ffn2_w_gate_up"][l, :, D_FF:], A["ffn2_w_down"][l])
            for l in range(DEPTH_2):
                linear(A["mod_w_2"][l], MOD_BLOCKS)
                ffn(A["ffn_w_gate_2"][l, 0], A["ffn_w_up_2"][l, 0], A["ffn_w_down_2"][l, 0])
                w = A["w_in_2"][l]
                heads(w[:, 0:P_A], H_A)
                linear(w, RWKV_BLOCKS)
                linear(w, HGRN_BLOCKS)
                for i, name in enumerate(("w_out_a_2", "w_out_b_2", "w_out_c_2")):
                    for lo, width in WO_BLOCKS:
                        linear(w, [(P_A + P_B + P_C + i * D + lo, width)])
                        linear(A[name][l], [(lo, width)])
                linear(A["w_out_2"][l], WO_BLOCKS)
                ffn(A["ffn_w_gate_2"][l, 1], A["ffn_w_up_2"][l, 1], A["ffn_w_down_2"][l, 1])

        @block.tensor
        def _(pe):
            n = Counts()

            def turn(kc):
                for g in range((kc + 1) // 2):
                    if g % 2 == 0:
                        ps, done, copied, k = turn_ps, tr_even, ev_even, n.even
                        n.even += 1
                    else:
                        ps, done, copied, k = aux_ps, tr_odd, ev_odd, n.odd
                        n.odd += 1
                    if k:
                        pe.wait_ge(copied, k)
                    for c in range(2 * g, min(2 * g + 2, kc)):
                        for t in range(NT):
                            at = ((c - 2 * g) * NT + t) * P
                            last = nc.tensor.transpose(ps[:, at:at + P], tok[:, t, c * P:(c + 1) * P], ident[:, :])
                    last.then_inc(done, 1)

            def turned():
                pe.wait_ge(ev_even, n.even)
                if n.odd:
                    pe.wait_ge(ev_odd, n.odd)

            def norm():
                pe.wait_ge(nm_scaled, n.scaled + 2)
                n.scaled += 2
                turn(KC)
                n.norm += 1

            def project(w, t, lhsT, rhs, kc, dmas=2):
                if t == 0:
                    pe.wait_ge(w_in[w.odd], n.dmas(w, dmas))
                for c in range(kc):
                    last = nc.tensor.matmul(proj_ps[t][:, 0:rhs.shape[2]], lhsT[:, c, t * P:(t + 1) * P],
                                            rhs[:, c, :], start=(c == 0), stop=(c == kc - 1))
                last.then_inc(proj_done, 1)

            def split_product(ps, lhsT, rhs, first, final):
                (a, a_lo), (b, b_lo) = lhsT, rhs
                nc.tensor.matmul(ps, rounded(a_lo), rounded(b), start=first, stop=False, skip_group_check=True)
                nc.tensor.matmul(ps, rounded(a), rounded(b_lo), start=False, stop=False, skip_group_check=True)
                return nc.tensor.matmul(ps, rounded(a), rounded(b), start=False, stop=final, skip_group_check=True)

            def ffn():
                def gate_up(st, w, t):
                    if st.s >= 1:
                        pe.wait_ge(ff_act, st.n(2, -1 + t))
                    if t == 0:
                        pe.wait_ge(cols_lo, st.n(1, 1))
                    lo, hi = (b[w.odd][:, :].rearrange("p (c n) -> p c n", c=KC) for b in (wproj_lo, wproj_hi))
                    toks = slice(t * P, (t + 1) * P)
                    for c in range(KC):
                        last = split_product(proj_ps[t][:, :], (x_hi(c)[:, toks], x_lo[:, c, toks]),
                                             (hi[:, c, :], lo[:, c, :]), c == 0, c == KC - 1)
                    last.then_inc(proj_done, 1)

                def turn_act(st):
                    pe.wait_ge(ff_act, st.n(2, 2))
                    if st.s >= 1:
                        pe.wait_ge(ff_copied, st.n())
                    for c in range(2):
                        for t in range(NT):
                            at = (c * NT + t) * P
                            last = nc.tensor.transpose(turn_ps[:, at:at + P], act_sb[:, t, c * P:(c + 1) * P],
                                                       ident[:, :])
                    last.then_inc(ff_turn, 1)

                def down(st, first, final):
                    pe.wait_ge(act_split, st.n(1, 1))
                    pe.wait_ge(rows_lo, st.n(1, 1))
                    for c in range(2):
                        for t in range(NT):
                            for h in range(2):
                                toks = slice((c * NT + t) * P, (c * NT + t + 1) * P)
                                outs = slice(h * 512, (h + 1) * 512)
                                last = split_product(down_ps[2 * t + h][:, :],
                                                     (actT_hi[st.odd][:, toks], actT_lo[st.odd][:, toks]),
                                                     (wdown_hi[st.odd][:, c, outs], wdown_lo[st.odd][:, c, outs]),
                                                     first and c == 0, final and c == 1)
                    last.then_inc(ff_down, 1)

                def step(st, w, first):
                    gate_up(st, w, 0)
                    turn_act(st.plus(-1))
                    gate_up(st, w, 1)
                    down(st.plus(-1), first, False)

                n.ffns += 1
                pe.wait_ge(x_split, n.ffns)
                gate_up(Step(n.ffn), Step(n.load), 0)
                gate_up(Step(n.ffn), Step(n.load), 1)
                step(Step(n.ffn + 1), Step(n.load + 1), True)
                step(Step(n.ffn + 2), Step(n.load + 2), False)
                with pe.Fori(0, (FF_STEPS - 3) // 2) as j:
                    for k in (3, 4):
                        step(Step(n.ffn + k, j), Step(n.load + k, j), False)
                n.ffn += FF_STEPS
                n.loaded(FF_STEPS, 0)
                turn_act(Step(n.ffn - 1))
                down(Step(n.ffn - 1), False, True)
                n.hidden += 1

            def linear(src, kc, blocks):
                turned()
                for lo, width in blocks:
                    w = Step(n.load)
                    rhs = wproj[w.odd][:, 0:kc * width].rearrange("p (c n) -> p c n", c=kc)
                    for t in range(NT):
                        if n.lin:
                            pe.wait_ge(ln_ev, 2 * n.lin - 1 + t)
                        project(w, t, src, rhs, kc)
                    n.loaded(1, 2)
                    n.lin += 1

            def attend(kind):
                heads_cat = kind == "mla"
                dk = MLA_QH if heads_cat else DH
                src = cat if heads_cat else qkv

                def project_pair(i, w, t):
                    if i.s >= 1:
                        pe.wait_ge(at_ev, i.n(2, -1 + t))
                    buf = wproj[w.odd]
                    if kind == "mla":
                        if t == 0:
                            pe.wait_ge(w_in[w.odd], n.dmas(w, 2))
                        wq = buf[:, 0:576].rearrange("p (c n) -> p c n", c=3)
                        wkv = buf[:, 576:1088].rearrange("p (c n) -> p c n", c=2)
                        for c in range(3):
                            nc.tensor.matmul(proj_ps[t][:, 0:192], xT[:, c, t * P:(t + 1) * P], wq[:, c, :],
                                             start=(c == 0), stop=(c == 2))
                        for c in range(2):
                            last = nc.tensor.matmul(proj_ps[t][:, 192:448], xT[:, 3 + c, t * P:(t + 1) * P],
                                                    wkv[:, c, :], start=(c == 0), stop=(c == 1))
                        last.then_inc(proj_done, 1)
                    else:
                        project(w, t, xT, buf[:, 0:KC * 384].rearrange("p (c n) -> p c n", c=KC), KC,
                                dmas=3)

                def turn_pair(i):
                    if kind == "sb":
                        pe.wait_ge(at_ev, i.n(2, 2))
                    else:
                        pe.wait_ge(at_prep, i.n(1, 1 - n.sb))
                    if i.s >= 1:
                        pe.wait_ge(at_turned, i.n())
                    if heads_cat:
                        for hd in range(2):
                            ps = (turn_ps, down_ps[2])[hd]
                            for s in range(2):
                                for t in range(NT):
                                    at = (s * NT + t) * P
                                    last = nc.tensor.transpose(ps[0:dk, at:at + P], cat[:, t, 2 * s + hd, :],
                                                               ident[:, :])
                    else:
                        for s in range(2):
                            for t in range(NT):
                                at = (s * NT + t) * P
                                last = nc.tensor.transpose(turn_ps[:, at:at + P],
                                                           qkv[i.odd][:, t, s * P:(s + 1) * P], ident[:, :])
                    last.then_inc(at_turn, 1)

                def scores(i, hd):
                    if hd == 0:
                        pe.wait_ge(at_turned, i.n(1, 1))
                    if i.s >= 1:
                        pe.wait_ge(at_l, i.n(2, -1 + hd))
                    if heads_cat:
                        m = qkT[0:dk, hd]
                    else:
                        m = qkT[DH * hd:DH * (hd + 1), 0]
                    for t in range(NT):
                        last = nc.tensor.matmul(down_ps[hd][:, t * SEQ:(t + 1) * SEQ], m[:, t * P:(t + 1) * P],
                                                m[:, SEQ:2 * SEQ], start=True, stop=True)
                    last.then_inc(at_s, 1)

                def turn_probs(i, hd):
                    pe.wait_ge(at_e, i.n(2, 1 + hd))
                    if i.s >= 1:
                        pe.wait_ge(at_ptc, i.n(2, -1 + hd))
                    for at, (t, kt) in enumerate(((0, 0), (1, 0), (1, 1))):
                        last = nc.tensor.transpose(down_ps[2 + hd][:, at * P:(at + 1) * P],
                                                   score[:, hd, t, kt * P:(kt + 1) * P], ident[:, :])
                    last.then_inc(at_pt, 1)

                def values(i, hd):
                    pe.wait_ge(at_ptc, i.n(2, 1 + hd))
                    if i.s >= 1 and hd == 0:
                        pe.wait_ge(at_o, i.n())
                    dv = P if kind == "diff" else DH
                    if kind == "mla":
                        v = [qkv[i.odd][:, t, 192 + P * hd + MLA_NOPE:192 + P * (hd + 1)] for t in range(NT)]
                    elif kind == "diff":
                        v = [qkv[i.odd][:, t, 256:384] for t in range(NT)]
                    else:
                        v = [qkv[i.odd][:, t, 256 + DH * hd:256 + DH * (hd + 1)] for t in range(NT)]
                    o = aux_ps[:, 0:4 * dv].rearrange("p (h t d) -> p h t d", h=2, t=NT)
                    nc.tensor.matmul(o[:, hd, 0], probT[:, hd, 0:P], v[0], start=True, stop=True)
                    nc.tensor.matmul(o[:, hd, 1], probT[:, hd, P:2 * P], v[0], start=True, stop=False)
                    nc.tensor.matmul(o[:, hd, 1], probT[:, hd, 2 * P:3 * P], v[1], start=False,
                                     stop=True).then_inc(at_pv, 1)

                def next_scores(i):
                    turn_pair(i)
                    scores(i, 0)
                    scores(i, 1)

                def weigh_values(i):
                    turn_probs(i, 0)
                    turn_probs(i, 1)
                    values(i, 0)
                    values(i, 1)

                def pair(i, w, more):
                    if more:
                        project_pair(i.plus(1), w.plus(1), 0)
                        project_pair(i.plus(1), w.plus(1), 1)
                    if more and kind == "sb":
                        next_scores(i.plus(1))
                    weigh_values(i)
                    if more and kind != "sb":
                        next_scores(i.plus(1))

                pairs = 4 if kind == "diff" else N_PAIRS
                turned()
                project_pair(Step(n.pair), Step(n.load), 0)
                project_pair(Step(n.pair), Step(n.load), 1)
                next_scores(Step(n.pair))
                run_steps(pe, pairs, 2, 2, lambda k, j:
                          pair(Step(n.pair + k, j), Step(n.load + k, j), k != pairs - 1))
                n.pair += pairs
                n.loaded(pairs, 2 if kind == "mla" else 3)
                if kind == "sb":
                    n.sb += pairs

            def out_proj(kc):
                pe.wait_ge(at_o, n.pair)
                turn(kc)
                linear(xT, kc, WO_BLOCKS)
                n.hidden += 1

            def mla():
                linear(xT, KC, MLA_BLOCKS)
                pe.wait_ge(nm_scaled, n.scaled + 2)
                n.scaled += 2
                turn(5)
                attend("mla")
                out_proj(KC)

            def project_f(blocks):
                for b, (lo, width) in enumerate(blocks):
                    w = Step(n.load)
                    slot = wproj[w.odd][:, 0:KC * width].rearrange("p (c n) -> p c n", c=KC)
                    for half in range(2):
                        if half == 0:
                            pe.wait_ge(w_in[w.odd], n.dmas(w, 2))
                        pe.wait_ge(ln_ev, 2 * n.lin - 1 + half)
                        for q in range(2 * half, 2 * half + 2):
                            m = min(P, width - q * P)
                            if m <= 0:
                                continue
                            for c in range(KC):
                                last = nc.tensor.matmul(
                                    proj_ps[half][0:m, (q % 2) * SEQ:(q % 2 + 1) * SEQ],
                                    slot[:, c, q * P:q * P + m], xT[:, c, :], start=(c == 0), stop=(c == KC - 1))
                        last.then_inc(proj_done, 1)
                    n.loaded(1, 2)
                    n.lin += 1

            def modulation():
                for lo, width in MOD_BLOCKS:
                    w = Step(n.load)
                    rhs = wproj[w.odd][:, :].rearrange("p (c n) -> p c n", c=KC)
                    for half in range(2):
                        if half == 0:
                            pe.wait_ge(w_in[w.odd], n.dmas(w, 2))
                        if n.lin:
                            pe.wait_ge(ln_ev, 2 * n.lin - 1 + half)
                        for c in range(KC):
                            last = nc.tensor.matmul(proj_ps[half][:, 0:256], condT[:, c, :],
                                                    rhs[:, c, half * 256:(half + 1) * 256],
                                                    start=(c == 0), stop=(c == KC - 1))
                        last.then_inc(proj_done, 1)
                    n.loaded(1, 2)
                    n.lin += 1

            def rwkv(l):
                project_f(RWKV_BLOCKS)
                pe.wait_ge(*rw_act.at(l, "lora_in"))
                pe.wait_ge(small_in, n.small)
                for c in range(BC):
                    dst = slice((c % 2) * SEQ, (c % 2 + 1) * SEQ)
                    cols = slice(c * P, (c + 1) * P)
                    nc.tensor.matmul(down_ps[c // 2][:, dst], lora_w[0:64, 0, cols], rw_xwa[0:64], start=True,
                                     stop=True)
                    nc.tensor.matmul(down_ps[2 + c // 2][:, dst], lora_w[64:128, 0, cols], rw_xwa[64:128],
                                     start=True, stop=True)
                    g_ps = (turn_ps, aux_ps)[c // 2]
                    nc.tensor.matmul(g_ps[:, dst], lora_w[:, 1, cols], rw_xg1[:], start=True, stop=False)
                    last = nc.tensor.matmul(g_ps[:, dst], lora_w[0:32, 2, cols], rw_xg2[0:32], start=False,
                                            stop=True)
                last.then_inc(*rw_pe.next("lora"))

                def head_sums():
                    for half in range(2):
                        last = nc.tensor.matmul(proj_ps[half][:, :], headsum[:, :],
                                                rw_t0[:, 2 * half:2 * half + 2].rearrange("p c s -> p (c s)"),
                                                start=True, stop=True)
                    return last

                def from_state(ps, c, which):
                    return nc.tensor.matmul(ps[:, c * P:(c + 1) * P], kr_in[:, c, which, :], state[:, c, :],
                                            start=True, stop=False)

                pe.wait_ge(*rw_v.at(l, "kk_sq"))
                head_sums().then_inc(*rw_pe.next("kk_ss"))
                pe.wait_ge(*rw_act.at(l, "lora_out"))
                for t in range(NT):
                    for c in range(BC):
                        last = nc.tensor.transpose(down_ps[t][:, c * P:(c + 1) * P], rw_v_[:, c, t * P:(t + 1) * P],
                                                   ident[:, :])
                last.then_inc(*rw_pe.next("vtok"))
                pe.wait_ge(*rw_v.at(l, "rk"))
                head_sums().then_inc(*rw_pe.next("bonus"))
                pe.wait_ge(*rw_v.at(l, "scaled"))
                for c in range(BC):
                    nc.tensor.transpose(down_ps[2][:, c * P:(c + 1) * P], k_end[:, c, :], ident[:, :])
                    last = nc.tensor.transpose(down_ps[3][:, c * P:(c + 1) * P], b_end[:, c, :], ident[:, :])
                last.then_inc(*rw_pe.next("kb_turn"))
                for t in range(NT):
                    for q in range(8):
                        if q == 0 and t == 0:
                            pe.wait_ge(*rw_act.at(l, "kb_c"))
                        if q == 0 and t == 1:
                            pe.wait_ge(*rw_v.at(l, "state_c"))
                        if q >= 4:
                            pe.wait_ge(*rw_v.at(l, f"mats{t}", q - 4))
                        c, base = q // 2, 64 * (q % 2)
                        ps = down_ps[q % 4][:, :].rearrange("p (a b n) -> p a b n", a=2, b=2)
                        rows = slice(base, base + 64)
                        for a, sources in enumerate(((kh, k1), (bh, b1))):
                            for blk, src in enumerate(sources):
                                lo = t * P + blk * BLK
                                last = nc.tensor.matmul(ps[:, a, :, blk * BLK:(blk + 1) * BLK],
                                                        src[rows, c, t * P:(t + 1) * P],
                                                        kr_all[rows, c, :, lo:lo + BLK], start=True, stop=True)
                        last.then_inc(*rw_pe.next(f"mat{t}"))
                    pe.wait_ge(*rw_v.at(l, f"xt{t}"))
                    for q in range(8):
                        last = nc.tensor.transpose((turn_ps, aux_ps)[q // 4][:, (q % 4) * P:(q % 4 + 1) * P],
                                                   invT[:, q, :], ident[:, :])
                    last.then_inc(*rw_pe.next(f"x0{t}"))
                    if t == 1:
                        pe.wait_ge(*rw_act.at(l, "oc0"))
                    for i in range(LV):
                        pe.wait_ge(*rw_v.at(l, f"x{t}", i))
                        pe.wait_ge(*rw_pool.at(l, f"et{t}", i))
                        for q in range(8):
                            last = nc.tensor.matmul(proj_ps[q // 4][:, (q % 4) * P:(q % 4 + 1) * P], part[:, q, :],
                                                    inv[:, q, :], start=True, stop=True)
                        last.then_inc(*rw_pe.next(f"yz{t}_{i}"))
                        pe.wait_ge(*rw_act.at(l, f"yc{t}", i))
                        for q in range(8):
                            cols = slice((q % 4) * P, (q % 4 + 1) * P)
                            if i < LV - 1:
                                nc.tensor.matmul(down_ps[q // 4][:, cols], invT[:, q, :], y_sb[:, q, :], start=True,
                                                 stop=True)
                            last = nc.tensor.matmul(down_ps[2 + q // 4][:, cols], y_sb[:, q, :], invT[:, q, :],
                                                    start=True, stop=True)
                        last.then_inc(*rw_pe.next(f"yz{t}_{i}"))
                    pe.wait_ge(*rw_v.at(l, f"x{t}", LV))
                    for q in range(8):
                        cols = slice(q * N_B, (q + 1) * N_B)
                        if t == 1 and q % 2 == 0:
                            from_state(turn_ps, q // 2, 0)
                        last = nc.tensor.matmul(turn_ps[:, cols], mats[:, q, 0, :], v_tok[:, t, cols], start=(t == 0),
                                                stop=(t == 0 or q % 2 == 1))
                    last.then_inc(*rw_pe.next(f"w{t}"))
                    pe.wait_ge(*rw_act.at(l, f"wc{t}"))
                    for q in range(8):
                        cols = slice(q * N_B, (q + 1) * N_B)
                        last = nc.tensor.matmul(aux_ps[:, cols], invT[:, q, :], w_tok[:, cols], start=True, stop=True)
                    last.then_inc(*rw_pe.next(f"u{t}"))
                    pe.wait_ge(*rw_v.at(l, f"un{t}"))
                    for q in range(8):
                        cols = slice(q * N_B, (q + 1) * N_B)
                        if t == 1 and q % 2 == 0:
                            from_state(proj_ps[t], q // 2, 1)
                        nc.tensor.matmul(proj_ps[t][:, cols], mats[:, q, 1, :], v_tok[:, t, cols], start=(t == 0),
                                         stop=False)
                        last = nc.tensor.matmul(proj_ps[t][:, cols], mats[:, q, 3, :], u_neg[:, cols], start=False,
                                                stop=(t == 0 or q % 2 == 1))
                    last.then_inc(*rw_pe.next(f"o{t}"))
                    if t == 0:
                        for c in range(BC):
                            cols = slice(c * P, (c + 1) * P)
                            nc.tensor.matmul(down_ps[0][:, cols], kb_tok[:, 0, cols], v_tok[:, 0, cols], start=True,
                                             stop=False)
                            last = nc.tensor.matmul(down_ps[0][:, cols], kb_tok[:, 1, cols], u_neg[:, cols],
                                                    start=False, stop=True)
                        last.then_inc(*rw_pe.next("state"))
                pe.wait_ge(*rw_v.at(l, "ln"))
                turn(BC)

            def hgrn(l):
                project_f(HGRN_BLOCKS[:2])
                linear(xT, KC, HGRN_BLOCKS[2:])
                pe.wait_ge(*hg_upd.at(l, "upd"))
                for q in range(8):
                    c, toks = q // 2, slice((q % 2) * P, (q % 2 + 1) * P)
                    last = nc.tensor.matmul(down_ps[q // 4][:, (q % 4) * P:(q % 4 + 1) * P], hk[:, c, toks],
                                            hq[:, c, toks], start=True, stop=True)
                last.then_inc(*hg_s.next("s"))
                for i in range(n_lv):
                    pe.wait_ge(*hg_x.at(l, "x", i))
                    if i >= 1:
                        pe.wait_ge(*hg_acc.at(l, "acc", i - 1))
                    x = h_x[i % 2]
                    banks = down_ps[2:4] if i % 2 == 0 else down_ps[0:2]
                    if i < len(LEVELS):
                        for q in range(8):
                            c, toks = q // 2, slice((q % 2) * P, (q % 2 + 1) * P)
                            last = nc.tensor.matmul(banks[q // 4][:, (q % 4) * P:(q % 4 + 1) * P], x[:, c, toks],
                                                    x[:, c, toks], start=True, stop=True)
                    else:
                        for c in range(BC):
                            last = nc.tensor.matmul(banks[0][:, c * P:(c + 1) * P], x[:, c, 0:P], x[:, c, P:SEQ],
                                                    start=True, stop=True)
                    last.then_inc(*hg_s.next("s"))
                pe.wait_ge(*hg_acc.at(l, "acc", n_lv))
                pe.wait_ge(ln_ev, 2 * n.lin)
                for t in range(NT):
                    for c in range(BC):
                        cols = slice(c * P, (c + 1) * P)
                        last = nc.tensor.matmul(proj_ps[t][:, cols], h_acc[:, 2 * c + t, :], h_v[:, t, cols],
                                                start=True, stop=(t == 0))
                        if t == 1:
                            last = nc.tensor.matmul(proj_ps[t][:, cols], h_cross[:, c, :], h_v[:, 0, cols],
                                                    start=False, stop=True)
                last.then_inc(*hg_o.next("o"))
                pe.wait_ge(*hg_out.at(l, "out"))
                turn(BC)

            def hybrid(l):
                attend("diff")
                pe.wait_ge(at_o, n.pair)
                turn(BC)
                rwkv(l)
                hgrn(l)
                for i in range(3):
                    for blk in WO_BLOCKS:
                        linear(xT, KC, [blk])
                        if i == 1:
                            pe.wait_ge(*rw_v.at(l, "out"))
                        linear(oT[i], BC, [blk])
                pe.wait_ge(y_ready, l + 1)
                turn(KC)
                linear(xT, KC, WO_BLOCKS)
                n.hidden += 1

            pe.wait_ge(masks_ready, 1)
            pe.wait_ge(vec_in, VEC_DMAS * DMA)
            for i, rows in enumerate(VEC_ROWS):
                dst = turn_ps[:, i * P:i * P + rows] if i < 4 else aux_ps[:, 0:rows]
                last = nc.tensor.transpose(dst, vec_row[0:rows, i, :], ident[0:rows, 0:rows])
            last.then_inc(vec_turned, 1)
            pe.wait_ge(vec_ready, 1)
            for l in range(DEPTH):
                norm()
                ffn()
                norm()
                if l % 3 == 2:
                    mla()
                else:
                    attend("sb" if l % 3 == 0 else "moba")
                    out_proj(KC)
                norm()
                ffn()
            n.scaled += 2
            for l in range(DEPTH_2):
                pe.wait_ge(condT_ready, l + 1)
                n.small += SMALL_DMAS * DMA
                modulation()
                norm()
                ffn()
                norm()
                hybrid(l)
                norm()
                ffn()

        @block.scalar
        def _(act):
            n = Counts()

            def norm():
                if n.hidden == 0:
                    act.wait_ge(x_in, DMA)
                else:
                    act.wait_ge(hid_ready, n.hidden)
                for t in range(NT):
                    nc.scalar.activation(tok[:, t, :], hid[:, t, :], ACT.Square,
                                         accum_out=sumsq[:, t:t + 1]).then_inc(nm_sq, 1)

            def round_columns(f, w):
                act.wait_ge(f_in[f.odd], f.half(2 * DMA, 2 * DMA))
                nc.scalar.copy(rounded(wproj_hi[w.odd][:, :]), wproj[w.odd][:, :]).then_inc(cols_hi, 1)

            def round_rows(f):
                act.wait_ge(d_in[f.odd], f.half(DMA, DMA))
                nc.scalar.copy(rounded(wdown_hi[f.odd][:]), wdown[f.odd][:]).then_inc(rows_rounded, 1)

            def copy_odd(kc, gain=None, bias=None, dst=xT, split=False):
                for g in range(1, (kc + 1) // 2, 2):
                    act.wait_ge(tr_odd, n.odd + 1)
                    for c in range(2 * g, min(2 * g + 2, kc)):
                        src = aux_ps[:, (c - 2 * g) * SEQ:(c - 2 * g + 1) * SEQ]
                        if split:
                            if bias is None:
                                nc.scalar.activation(rounded(x_hi(c)), src, ACT.Copy, scale=gain(c))
                            else:
                                nc.scalar.activation(rounded(x_hi(c)), src, ACT.Identity, scale=gain(c), bias=bias(c))
                        if gain is None:
                            last = nc.scalar.copy(dst[:, c, :], src)
                        elif bias is None:
                            last = nc.scalar.activation(dst[:, c, :], src, ACT.Copy, scale=gain(c))
                        else:
                            last = nc.scalar.activation(dst[:, c, :], src, ACT.Identity, scale=gain(c), bias=bias(c))
                    last.then_inc(ev_odd, 1)
                    n.odd += 1

            def ffn(gain, bias=None):
                def step(k, st, w):
                    for t in range(NT):
                        act.wait_ge(proj_done, w.n(2, 1 + t))
                        if st.s >= 1:
                            act.wait_ge(ff_act, st.n(2, -1 + t))
                        nc.scalar.activation(gate_sb[:, t, :], proj_ps[t][:, 0:FFB], ACT.Silu).then_inc(ff_silu, 1)
                    round_rows(st)
                    act.wait_ge(ff_turn, st.n(1, 1))
                    if st.s >= 2:
                        act.wait_ge(ff_down, st.n(1, -1))
                    nc.scalar.copy(actT[st.odd][:, :], turn_ps[:, :])
                    nc.scalar.copy(rounded(actT_hi[st.odd][:, :]), turn_ps[:, :]).then_inc(ff_copied, 1)
                    if k + 2 < FF_STEPS:
                        round_columns(st.plus(2), w.plus(2))

                norm()
                round_columns(Step(n.ffn), Step(n.load))
                copy_odd(KC, gain, bias, split=True)
                round_columns(Step(n.ffn + 1), Step(n.load + 1))
                run_steps(act, FF_STEPS, 3, 2, lambda k, j: step(k, Step(n.ffn + k, j), Step(n.load + k, j)))
                n.ffn += FF_STEPS
                n.load += FF_STEPS

            def attend(kind):
                def evac(i, w, t):
                    act.wait_ge(proj_done, w.n(2, 1 + t))
                    if i.s >= 2:
                        act.wait_ge(at_pv, i.n(2, -2))
                    width = 448 if kind == "mla" else 384
                    nc.scalar.copy(qkv[i.odd][:, t, 0:width], proj_ps[t][:, 0:width]).then_inc(at_ev, 1)

                def copy_qk(i):
                    act.wait_ge(at_turn, i.n(1, 1))
                    if i.s >= 1:
                        act.wait_ge(at_s, i.n(2))
                    if kind == "mla":
                        nc.scalar.copy(qkT[0:MLA_QH, 0, :], turn_ps[0:MLA_QH, :])
                        last = nc.scalar.copy(qkT[0:MLA_QH, 1, :], down_ps[2][0:MLA_QH, :])
                    else:
                        last = nc.scalar.copy(qkT[:, 0, :], turn_ps[:, :])
                    last.then_inc(at_turned, 1)

                def weights(i, u, hd):
                    act.wait_ge(at_l, i.n(2, 1 + hd))
                    if kind == "sb":
                        if u.s >= 1:
                            act.wait_ge(sb_arg, u.n(2, -1 + hd))
                        nc.scalar.activation(soft[:, hd], score[:, hd], ACT.Abs)
                        act.drain()
                        nc.scalar.activation(soft[:, hd], soft[:, hd], ACT.Exp, scale=-1.0)
                        act.drain()
                        nc.scalar.activation(soft[:, hd], soft[:, hd], ACT.Ln, bias=1.0).then_inc(sb_soft, 1)
                    else:
                        if i.s >= 1:
                            act.wait_ge(at_o, i.n())
                        for t in range(NT):
                            last = nc.scalar.activation(score[:, hd, t], score[:, hd, t], ACT.Exp,
                                                        bias=negmax[:, hd, t:t + 1],
                                                        accum_out=rowsum[:, hd, t:t + 1])
                        last.then_inc(at_e, 1)

                def exp_arg(i, u, hd):
                    act.wait_ge(sb_arg, u.n(2, 1 + hd))
                    nc.scalar.activation(score[:, hd], score[:, hd], ACT.Exp).then_inc(at_e, 1)

                def copy_pt(i, hd):
                    act.wait_ge(at_pt, i.n(2, 1 + hd))
                    if i.s >= 1:
                        act.wait_ge(at_pv, i.n(2, -1 + hd))
                    nc.scalar.copy(probT[:, hd, :], down_ps[2 + hd][:, 0:384]).then_inc(at_ptc, 1)

                def pair(i, w, u, more):
                    weights(i, u, 0)
                    weights(i, u, 1)
                    if more:
                        evac(i.plus(1), w.plus(1), 0)
                        evac(i.plus(1), w.plus(1), 1)
                    if kind == "sb":
                        if more:
                            copy_qk(i.plus(1))
                        exp_arg(i, u, 0)
                        exp_arg(i, u, 1)
                    copy_pt(i, 0)
                    copy_pt(i, 1)
                    if more and kind != "sb":
                        copy_qk(i.plus(1))

                pairs = 4 if kind == "diff" else N_PAIRS
                evac(Step(n.pair), Step(n.load), 0)
                evac(Step(n.pair), Step(n.load), 1)
                copy_qk(Step(n.pair))
                run_steps(act, pairs, 2, 2, lambda k, j:
                          pair(Step(n.pair + k, j), Step(n.load + k, j), Step(n.sb + k, j), k != pairs - 1))
                n.pair += pairs
                n.load += pairs
                if kind == "sb":
                    n.sb += pairs

            def skip_linear(blocks):
                n.load += len(blocks)
                n.lin += len(blocks)

            def out_proj(kc):
                copy_odd(kc)
                skip_linear(WO_BLOCKS)
                n.hidden += 1

            def mla():
                for b, (lo, width) in enumerate(MLA_BLOCKS):
                    for t in range(NT):
                        act.wait_ge(proj_done, 2 * n.load + 1 + t)
                        nc.scalar.copy(mla_c[:, t, lo:lo + width], proj_ps[t][:, 0:width]).then_inc(ln_ev, 1)
                    n.load += 1
                    n.lin += 1
                act.drain()
                for t in range(NT):
                    for s, (lo, width) in enumerate(((0, MLA_Q_RANK), (MLA_Q_RANK, MLA_KV_RANK))):
                        last = nc.scalar.activation(tok[:, t, lo:lo + width], mla_c[:, t, lo:lo + width],
                                                    ACT.Square, accum_out=sumsq[:, 2 * s + t:2 * s + t + 1])
                    last.then_inc(nm_sq, 1)
                n.sq += 2
                copy_odd(5, lambda c: mla_gains[:, c:c + 1])
                attend("mla")
                out_proj(KC)

            def rwkv(l):
                for b, (lo, width) in enumerate(RWKV_BLOCKS):
                    for half in range(2):
                        act.wait_ge(proj_done, 2 * n.load + 1 + half)
                        for q, dst in shift_places(b, half):
                            m = min(P, width - (2 * half + q) * P)
                            at = 4 * b + 2 * half + q
                            last = nc.scalar.activation(dst[0:m], proj_ps[half][0:m, q * SEQ:(q + 1) * SEQ],
                                                        ACT.Copy, scale=one_less[0:m, at:at + 1])
                        last.then_inc(shift_part, 1)
                    n.load += 1
                    n.lin += 1
                act.wait_ge(ln_ev, 2 * n.lin)
                nc.scalar.activation(rw_xwa[0:64], rw_xwa[0:64], ACT.Tanh)
                nc.scalar.activation(rw_xg1[:], rw_xg1[:], ACT.Sigmoid)
                nc.scalar.activation(rw_xg2[0:32], rw_xg2[0:32], ACT.Sigmoid).then_inc(*rw_act.next("lora_in"))
                act.wait_ge(*rw_pe.at(l, "lora"))
                w0, a0 = VEC_2["w0"], VEC_2["a0"]
                for c in range(BC):
                    src = slice((c % 2) * SEQ, (c % 2 + 1) * SEQ)
                    nc.scalar.activation(rw_t1[:, c], down_ps[c // 2][:, src], ACT.Sigmoid,
                                         bias=vec[:, 1 + l, w0 + c:w0 + c + 1])
                    nc.scalar.activation(rw_a[:, c], down_ps[2 + c // 2][:, src], ACT.Sigmoid,
                                         bias=vec[:, 1 + l, a0 + c:a0 + c + 1])
                for half, ps in enumerate((turn_ps, aux_ps)):
                    last = nc.scalar.copy(oT[2][:, 2 * half:2 * half + 2].rearrange("p c s -> p (c s)"), ps[:, :])
                last.then_inc(*rw_act.next("lora_out"))
                act.wait_ge(*rw_pe.at(l, "kk_ss"))
                for half in range(2):
                    last = nc.scalar.activation(rw_t2[:, 2 * half:2 * half + 2].rearrange("p c s -> p (c s)"),
                                                proj_ps[half][:, :], ACT.Sqrt)
                last.then_inc(*rw_act.next("kk_norm"))
                act.wait_ge(*rw_pe.at(l, "vtok"))
                for t in range(NT):
                    last = nc.scalar.copy(v_tok[:, t, :], down_ps[t][:, :])
                last.then_inc(*rw_act.next("vtok_c"))
                act.wait_ge(*rw_v.at(l, "expo"))
                nc.scalar.activation(kr_all[:, :, 0], kr_all[:, :, 0], ACT.Exp)
                nc.scalar.activation(kr_all[:, :, 1], rw_p, ACT.Exp)
                nc.scalar.activation(kh, rw_p, ACT.Exp, scale=-1.0)
                nc.scalar.activation(k1, k1, ACT.Exp)
                nc.scalar.activation(kr_in, kr_in, ACT.Exp)
                nc.scalar.activation(k_end, k_end, ACT.Exp).then_inc(*rw_act.next("exps"))
                act.wait_ge(*rw_pe.at(l, "kb_turn"))
                nc.scalar.copy(kb_tok[:, 0], down_ps[2][:, :])
                nc.scalar.copy(kb_tok[:, 1], down_ps[3][:, :]).then_inc(*rw_act.next("kb_c"))
                for t in range(NT):
                    for i in range(LV):
                        act.wait_ge(*rw_pe.at(l, f"yz{t}_{i}"))
                        for half in range(2):
                            last = nc.scalar.copy(y_sb[:, 4 * half:4 * half + 4].rearrange("p q n -> p (q n)"),
                                                  proj_ps[half][:, :])
                        last.then_inc(*rw_act.next(f"yc{t}"))
                    act.wait_ge(*rw_pe.at(l, f"w{t}"))
                    nc.scalar.copy(w_tok, turn_ps[:, :]).then_inc(*rw_act.next(f"wc{t}"))
                    act.wait_ge(*rw_pe.at(l, f"o{t}"))
                    nc.scalar.copy(tok[:, t, 0:W_B], proj_ps[t][:, :]).then_inc(*rw_act.next(f"oc{t}"))
                w, b = VEC_2["ln_w"], VEC_2["ln_b"]
                copy_odd(BC, lambda c: vec[:, 1 + l, w + c:w + c + 1], lambda c: vec[:, 1 + l, b + c:b + c + 1], oT[1])

            def hgrn(l):
                for b in range(4):
                    for t in range(2):
                        act.wait_ge(proj_done, 2 * n.load + 1 + t)
                        pair = slice(2 * t, 2 * t + 2)
                        flat = "p c s -> p (c s)"
                        if b == 0:
                            last = nc.scalar.activation(hq[:, pair].rearrange(flat), proj_ps[t][:, :], ACT.Silu)
                        elif b == 1:
                            nc.scalar.activation(hk[:, pair].rearrange(flat), proj_ps[t][:, :], ACT.Sigmoid, scale=-1.0)
                            last = nc.scalar.copy(hf[:, pair].rearrange(flat), proj_ps[t][:, :])
                        elif b == 2:
                            last = nc.scalar.copy(h_v[:, t], proj_ps[t][:, :])
                        else:
                            last = nc.scalar.activation(h_g[:, t], proj_ps[t][:, :], ACT.Silu)
                        last.then_inc(ln_ev, 1)
                    n.load += 1
                    n.lin += 1
                passes = [(hg_abs.at(l, "abs"), hg_ln.next("ln"))]
                if l > 0:
                    passes.append((hb_abs.at(0, "abs"), hb_ln.next("ln")))
                for wait, done in passes:
                    act.wait_ge(*wait)
                    nc.scalar.activation(h_t, h_t, ACT.Exp, scale=-1.0)
                    act.drain()
                    nc.scalar.activation(h_t, h_t, ACT.Ln, bias=1.0).then_inc(*done)
                for i, m in enumerate(LEVELS + [P]):
                    act.wait_ge(*hg_upd.at(l, "upd", i))
                    if i >= 1:
                        act.wait_ge(*hg_x.at(l, "x", i - 1))
                    e, f, g = (halves(x, m) for x in (h_e, hf, hs))
                    nc.scalar.activation(e[:, :, 1], f[:, :, 1], ACT.Exp)
                    nc.scalar.activation(e[:, :, 0], g[:, :, 0], ACT.Exp).then_inc(*hg_ex.next("ex"))
                act.wait_ge(*hg_o.at(l, "o"))
                for t in range(NT):
                    last = nc.scalar.copy(tok[:, t, 0:W_C], proj_ps[t][:, :])
                last.then_inc(*hg_oc.next("oc"))
                w = VEC_2["hnorm"]
                copy_odd(BC, lambda c: vec[:, 1 + l, w:w + 1], None, oT[2])

            def hybrid(l):
                attend("diff")
                copy_odd(BC, lambda c: vec[:, 1 + l, VEC_2["subln"]:VEC_2["subln"] + 1], None, oT[0])
                rwkv(l)
                hgrn(l)
                for i in range(3):
                    for lo, width in WO_BLOCKS:
                        for t in range(NT):
                            if t == 0:
                                act.wait_ge(ln_ev, 2 * n.lin)
                            act.wait_ge(proj_done, 2 * n.load + 1 + t)
                            nc.scalar.activation(gate[:, t, :], proj_ps[t][:, :], ACT.Sigmoid).then_inc(ln_ev, 1)
                        n.load += 2
                        n.lin += 2
                copy_odd(KC)
                skip_linear(WO_BLOCKS)
                n.hidden += 1

            def row(i, at, vector):
                rows = vector.shape[0] // P
                act.dma_start(vec_row[at:at + rows, i, :], vector.rearrange("(r f) -> r f", f=P)).then_inc(vec_in, DMA)

            act.wait_ge(masks_ready, 1)
            for l in range(DEPTH):
                for s, name in enumerate(("norm_ffn1", "norm_mix", "norm_ffn2")):
                    row(0, (3 * l + s) * KC, A[name][l])
            row(0, VEC_1["q_norm"], A["mla_q_norm"][0])
            row(0, VEC_1["kv_norm"], A["mla_kv_norm"][0])
            row(0, VEC_1["c"], A["c_2"][0])
            row(0, VEC_1["index"], A["token_index"])
            for l in range(DEPTH_2):
                whole = 14 * P
                row(1 + l, VEC_2["mu"], A["rwkv_mu_2"][l, 0:whole])
                act.dma_start(vec_row[VEC_2["mu"] + 14:VEC_2["mu"] + 15, 1 + l, 0:P_B - whole],
                              A["rwkv_mu_2"][l:l + 1, whole:P_B]).then_inc(vec_in, DMA)
                for name in ("w0", "a0", "k_k", "k_a", "ln_w", "ln_b"):
                    row(1 + l, VEC_2[name], A[f"rwkv_{name}_2"][l])
                row(1 + l, VEC_2["r_k"], A["rwkv_r_k_2"][l].rearrange("h n -> (h n)"))
                row(1 + l, VEC_2["subln"], A["subln_w_2"][l])
                row(1 + l, VEC_2["hnorm"], A["hgrn_norm_w_2"][l])
                for k in range(DEPTH_2):
                    row(1 + l, VEC_2[f"bound{k}"], A["hgrn_lower_bounds_2"][k])
                row(1 + l, VEC_2["norm_w"], A["norm_w_2"][l].rearrange("a b -> (a b)"))
                row(3 + l, 0, A["mod_b_2"][l])
            with nc.allow_non_contiguous_dma("256 positions, once"):
                act.dma_start(pos_i[:, :], A["positions_2"].rearrange("b (t p) -> p (b t)", p=P)).then_inc(const_in, DMA)
            act.dma_start(grow[:, :], A["final_norm"].rearrange("(a d) -> a d", a=1).broadcast_to([P, D])).then_inc(const_in, DMA)
            act.dma_start(freq[:, :], A["rope_freq"].rearrange("(a d) -> a d", a=1).broadcast_to([P, NROPE])).then_inc(const_in, DMA)
            act.dma_start(qkw[:].rearrange("p a b c -> p (a b c)"), A["qk_norm_w_2"].rearrange("a b c -> (a b c)").unsqueeze(0)
                          .broadcast_to([P, DEPTH_2 * 2 * DH_A])).then_inc(const_in, DMA)
            act.dma_start(lqk[:].rearrange("p a b c -> p (a b c)"), A["lambda_qk_2"].rearrange("a b c -> (a b c)").unsqueeze(0)
                          .broadcast_to([P, DEPTH_2 * 4 * DH_A])).then_inc(const_in, DMA)
            act.wait_ge(const_in, CONST_DMAS * DMA)
            act.wait_ge(trig_ang, 1)
            nc.scalar.activation(trig[:], ang[:], ACT.Sin).then_inc(trig_ready, 1)
            act.wait_ge(vec_ready, 1)
            nc.scalar.activation(cond[:, :], vec[:, 0, VEC_1["c"]:VEC_1["c"] + KC], ACT.Silu).then_inc(cond_ready, 1)
            act.wait_ge(lam_terms, 1)
            nc.scalar.activation(lam_e[:], lam_e[:], ACT.Exp).then_inc(lam_exp, 1)
            act.wait_ge(low_d, 1)
            nc.scalar.activation(lows[:, 3], lows[:, 3], ACT.Exp, scale=-1.0)
            act.drain()
            nc.scalar.activation(lows[:, 3], lows[:, 3], ACT.Ln, bias=1.0).then_inc(low_s, 1)
            act.wait_ge(low_d, 2)
            nc.scalar.activation(lows[:, 2], lows[:, 1], ACT.Exp).then_inc(low_s, 1)

            def gained(k):
                return lambda c: gains[:, k, c:c + 1]

            def first_stack():
                for l in range(DEPTH):
                    ffn(gained(3 * l))
                    n.hidden += 1
                    norm()
                    copy_odd(KC, gained(3 * l + 1))
                    if l % 3 == 2:
                        mla()
                    else:
                        attend("sb" if l % 3 == 0 else "moba")
                        out_proj(KC)
                    ffn(gained(3 * l + 2))
                    n.hidden += 1

            def modulated(k):
                return lambda c: modA[:, k, c:c + 1], lambda c: modcol[:, 3 * k * KC + c:3 * k * KC + c + 1]

            first_stack()
            norm()
            n.hidden += 1
            for l in range(DEPTH_2):
                act.wait_ge(hid_ready, n.hidden)
                for dst, src in ((lora_w[0:R_W, 0, :], A["rwkv_w2_2"][l]), (lora_w[R_W:P, 0, :], A["rwkv_a2_2"][l]),
                                 (lora_w[:, 1, :], A["rwkv_g2_2"][l, 0:P]), (lora_w[0:R_G - P, 2, :], A["rwkv_g2_2"][l, P:R_G])):
                    act.dma_start(dst, src).then_inc(small_in, DMA)
                for k in range(3):
                    src = A["mod_b_2"][l:l + 1, (3 * k + 2) * D:(3 * k + 3) * D]
                    act.dma_start(modrow[:, k, :], src.broadcast_to([P, D])).then_inc(small_in, DMA)
                skip_linear(MOD_BLOCKS)
                ffn(*modulated(0))
                n.hidden += 1
                norm()
                copy_odd(KC, *modulated(1))
                hybrid(l)
                ffn(*modulated(2))
                n.hidden += 1
            act.wait_ge(hid_ready, n.hidden)
            act.dma_start(out.rearrange("b (t p) d -> p (b t) d", p=P), hid[:]).then_inc(out_done, DMA)
            act.wait_ge(out_done, DMA)

        @block.vector
        def _(v):
            n = Counts()
            V = nc.vector

            def rest_of_columns(f, w):
                v.wait_ge(cols_hi, f.n(1, 1))
                V.tensor_tensor(rounded(wproj_lo[w.odd][:, :]), wproj[w.odd][:, :], wproj_hi[w.odd][:, :],
                                ALU.subtract).then_inc(cols_lo, 1)

            def rest_of_rows(f):
                v.wait_ge(rows_rounded, f.n(1, 1))
                V.tensor_tensor(rounded(wdown_lo[f.odd][:]), wdown[f.odd][:], wdown_hi[f.odd][:],
                                ALU.subtract).then_inc(rows_lo, 1)

            def copy_even(kc, gain=None, bias=None, dst=xT, split=False):
                for g in range(0, (kc + 1) // 2, 2):
                    v.wait_ge(tr_even, n.even + 1)
                    for c in range(2 * g, min(2 * g + 2, kc)):
                        src = turn_ps[:, (c - 2 * g) * SEQ:(c - 2 * g + 1) * SEQ]
                        if split:
                            if bias is None:
                                V.tensor_scalar(rounded(x_hi(c)), src, gain(c), None, ALU.mult)
                            else:
                                V.tensor_scalar(rounded(x_hi(c)), src, gain(c), bias(c), ALU.mult, ALU.add)
                        if gain is None:
                            last = V.tensor_copy(dst[:, c, :], src)
                        elif bias is None:
                            last = V.tensor_scalar(dst[:, c, :], src, gain(c), None, ALU.mult)
                        else:
                            last = V.tensor_scalar(dst[:, c, :], src, gain(c), bias(c), ALU.mult, ALU.add)
                    last.then_inc(ev_even, 1)
                    n.even += 1
                n.odd += (kc + 1) // 2 // 2

            def norm():
                n.rstd += 1
                v.wait_ge(rstd_ready, n.rstd)
                for t in range(NT):
                    V.tensor_scalar(tok[:, t, :], hid[:, t, :], rstd[:, t:t + 1], None,
                                    ALU.mult).then_inc(nm_scaled, 1)

            def ffn(gain, bias=None, row=None):
                def step(k, st, w):
                    for t in range(NT):
                        v.wait_ge(ff_silu, st.n(2, 1 + t))
                        if st.s >= 1:
                            v.wait_ge(ff_turn, st.n())
                        V.tensor_tensor(act_sb[:, t, :], gate_sb[:, t, :], proj_ps[t][:, FFB:2 * FFB],
                                        ALU.mult).then_inc(ff_act, 1)
                    rest_of_rows(st)
                    v.wait_ge(ff_copied, st.n(1, 1))
                    V.tensor_tensor(rounded(actT_lo[st.odd][:, :]), actT[st.odd], actT_hi[st.odd][:, :],
                                    ALU.subtract).then_inc(act_split, 1)
                    if k + 2 < FF_STEPS:
                        rest_of_columns(st.plus(2), w.plus(2))

                norm()
                rest_of_columns(Step(n.ffn), Step(n.load))
                copy_even(KC, gain, bias, split=True)
                n.ffns += 1
                v.drain()
                v.wait_ge(ev_odd, n.odd)
                for half in range(2):
                    chunks = slice(half * BC, (half + 1) * BC)
                    last = V.tensor_tensor(rounded(x_lo[:, chunks, :]), xT[:, chunks, :], x_hi_parts[half][:],
                                           ALU.subtract)
                last.then_inc(x_split, 1)
                rest_of_columns(Step(n.ffn + 1), Step(n.load + 1))
                run_steps(v, FF_STEPS, 3, 2, lambda k, j: step(k, Step(n.ffn + k, j), Step(n.load + k, j)))
                n.ffn += FF_STEPS
                n.load += FF_STEPS
                v.wait_ge(ff_down, n.ffn)
                for t in range(NT):
                    for h in range(2):
                        cols = slice(h * 512, (h + 1) * 512)
                        if row is not None:
                            V.tensor_tensor(tok[:, t, cols], down_ps[2 * t + h][:, :], modrow[:, row, cols],
                                            ALU.mult)
                        else:
                            last = V.scalar_tensor_tensor(hid[:, t, cols], down_ps[2 * t + h][:, :], 0.5,
                                                          hid[:, t, cols], ALU.mult, ALU.add)
                if row is not None:
                    v.drain()
                    last = V.tensor_tensor(hid[:], hid[:], tok[:], ALU.add)
                last.then_inc(hid_ready, 1)
                n.hidden += 1

            def rotate(x1, x2, y1, y2, m, f0, nf):
                shape = [P, NT, m, nf]
                c = cos_t[:, :, f0:f0 + nf].unsqueeze(2).broadcast_to(shape)
                s = sin_t[:, :, f0:f0 + nf].unsqueeze(2).broadcast_to(shape)
                r = [rt[:, q, 0:NT * m * nf].rearrange("p (t m f) -> p t m f", t=NT, m=m) for q in range(4)]
                V.tensor_tensor(r[0], x1, c, ALU.mult)
                V.tensor_tensor(r[1], x2, s, ALU.mult)
                V.tensor_tensor(r[2], x1, s, ALU.mult)
                V.tensor_tensor(r[3], x2, c, ALU.mult)
                v.drain()
                V.tensor_tensor(y1, r[0], r[1], ALU.subtract)
                return V.tensor_tensor(y2, r[2], r[3], ALU.add)

            def attend(kind, layer=None):
                scale = MLA_QH ** -0.5 if kind == "mla" else DH ** -0.5

                def prepare(i):
                    if kind == "sb":
                        return
                    v.wait_ge(at_ev, i.n(2, 2))
                    if kind == "diff":
                        x = qkv[i.odd][:, :, 0:256].rearrange("p t (m d) -> p t m d", d=DH_A)
                        sq = rt[:, 0:2].rearrange("p a b -> p (a b)").rearrange("p (t m d) -> p t m d", t=NT, m=4)
                        V.tensor_tensor(sq, x, x, ALU.mult)
                        v.drain()
                        V.tensor_reduce(heads_ss[:].rearrange("p (t m) -> p t m", t=NT), sq, AX.X,
                                        ALU.add).then_inc(head_ss, 1)
                        n.diff += 1
                        v.wait_ge(head_rs, n.diff)
                        V.tensor_tensor(x, x, heads_rs[:].rearrange("p (t m) -> p t m", t=NT).unsqueeze(3)
                                        .broadcast_to([P, NT, 4, DH_A]), ALU.mult)
                        v.drain()
                        for s in range(2):
                            y = x[:, :, 2 * s:2 * s + 2]
                            V.tensor_tensor(y, y, qkw[:, layer, s, :].unsqueeze(1).unsqueeze(1)
                                            .broadcast_to([P, NT, 2, DH_A]), ALU.mult)
                        v.drain()
                        x1, x2 = x[:, :, :, 0:DH_A // 2], x[:, :, :, DH_A // 2:DH_A]
                        last = rotate(x1, x2, x1, x2, 4, ROT_DIM // 2 + MLA_ROPE // 2, DH_A // 2)
                    elif kind == "moba":
                        x = qkv[i.odd][:, :, 0:256].rearrange("p t (m d) -> p t m d", d=DH)
                        half = ROT_DIM // 2
                        x1, x2 = x[:, :, :, 0:half], x[:, :, :, half:ROT_DIM]
                        last = rotate(x1, x2, x1, x2, 4, 0, half)
                    else:
                        half = MLA_ROPE // 2
                        if i.s >= 1:
                            v.wait_ge(at_turn, i.n())
                        q = qkv[i.odd][:, :, 0:192].rearrange("p t (m d) -> p t m d", d=MLA_QH)
                        k = qkv[i.odd][:, :, 192:448].rearrange("p t (m d) -> p t m d", d=P)
                        V.tensor_copy(cat[:, :, 0:2, 0:MLA_NOPE], q[:, :, :, 0:MLA_NOPE])
                        V.tensor_copy(cat[:, :, 2:4, 0:MLA_NOPE], k[:, :, :, 0:MLA_NOPE])
                        V.tensor_copy(cat[:, :, 2:4, MLA_NOPE:MLA_QH],
                                      kr_sb[:, :, :].unsqueeze(2).broadcast_to([P, NT, 2, MLA_ROPE]))
                        last = rotate(q[:, :, :, MLA_NOPE:MLA_NOPE + half], q[:, :, :, MLA_NOPE + half:MLA_QH],
                                      cat[:, :, 0:2, MLA_NOPE:MLA_NOPE + half],
                                      cat[:, :, 0:2, MLA_NOPE + half:MLA_QH], 2, ROT_DIM // 2, half)
                    last.then_inc(at_prep, 1)

                def logits(i, u, hd):
                    v.wait_ge(at_s, i.n(2, 1 + hd))
                    if i.s >= 1:
                        v.wait_ge(at_pt, i.n(2, -1 + hd))
                    flat = "p t k -> p (t k)"
                    s = score[:, hd].rearrange(flat)
                    if kind == "sb":
                        V.tensor_scalar(s, down_ps[hd][:, :], scale, None, ALU.mult).then_inc(at_l, 1)
                    else:
                        V.scalar_tensor_tensor(s, down_ps[hd][:, :], scale, causal[:].rearrange(flat),
                                               ALU.mult, ALU.add)
                        v.drain()
                        V.tensor_reduce(negmax[:, hd], score[:, hd], AX.X, ALU.max, negate=True).then_inc(at_l, 1)

                def stick(i, u, hd):
                    v.wait_ge(sb_soft, u.n(2, 1 + hd))
                    flat = "p t k -> p (t k)"
                    s, f = score[:, hd].rearrange(flat), soft[:, hd].rearrange(flat)
                    V.scalar_tensor_tensor(f, s, 0.0, f, ALU.max, ALU.add)
                    v.drain()
                    V.tensor_tensor(f, f, past01[:].rearrange(flat), ALU.mult)
                    V.tensor_tensor(s, s, pastneg[:].rearrange(flat), ALU.add)
                    v.drain()
                    for t in range(NT):
                        V.tensor_tensor_scan(soft[:, hd, t, ::-1], ones[:, :], soft[:, hd, t, ::-1], 0.0,
                                             ALU.mult, ALU.add)
                    v.drain()
                    V.tensor_tensor(s, s, f, ALU.subtract).then_inc(sb_arg, 1)

                def outputs(i, c):
                    v.wait_ge(at_pv, i.n(2, 2))
                    if kind == "diff":
                        V.reciprocal(rinv[:], rowsum[:])
                        v.drain()
                        V.tensor_scalar(rinv[:, 1], rinv[:, 1], lam[:, layer:layer + 1], None, ALU.mult)
                        v.drain()
                        V.tensor_tensor(o_head[:, 0:2], aux_ps[:, :].rearrange("p (h t d) -> p h t d", h=2, t=NT),
                                        rinv[:].unsqueeze(3).broadcast_to([P, 2, NT, P]), ALU.mult)
                        v.drain()
                        V.tensor_tensor(o_head[:, 0], o_head[:, 0], o_head[:, 1], ALU.subtract)
                        v.drain()
                        V.tensor_tensor(o_head[:, 2], o_head[:, 0], o_head[:, 0], ALU.mult)
                        v.drain()
                        V.tensor_reduce(heads_ss[:, 0:2], o_head[:, 2], AX.X, ALU.add).then_inc(head_ss, 1)
                        n.diff += 1
                        v.wait_ge(head_rs, n.diff)
                        V.tensor_tensor(tok[:, :, bass.ds(c.n(P), P)], o_head[:, 0],
                                        heads_rs[:, 0:2].unsqueeze(2).broadcast_to([P, NT, P]),
                                        ALU.mult).then_inc(at_o, 1)
                        return
                    dst = tok[:, :, bass.ds(c.n(P), P)].rearrange("p t (h d) -> p h t d", h=2)
                    src = aux_ps[:, 0:SEQ].rearrange("p (h t d) -> p h t d", h=2, t=NT)
                    if kind == "sb":
                        V.tensor_copy(dst, src).then_inc(at_o, 1)
                    else:
                        V.reciprocal(rinv[:], rowsum[:])
                        v.drain()
                        V.tensor_tensor(dst, src, rinv[:].unsqueeze(3).broadcast_to([P, 2, NT, DH]),
                                        ALU.mult).then_inc(at_o, 1)

                def pair(i, u, c, k):
                    logits(i, u, 0)
                    logits(i, u, 1)
                    if kind == "sb":
                        if k > 0:
                            outputs(i.plus(-1), c.plus(-1))
                        stick(i, u, 0)
                        stick(i, u, 1)
                        if k == pairs - 1:
                            outputs(i, c)
                    else:
                        if k != pairs - 1:
                            prepare(i.plus(1))
                        outputs(i, c)

                pairs = 4 if kind == "diff" else N_PAIRS
                prepare(Step(n.pair))
                run_steps(v, pairs, 2, 2, lambda k, j: pair(Step(n.pair + k, j), Step(n.sb + k, j), Step(k, j), k))
                n.pair += pairs
                n.load += pairs
                if kind == "sb":
                    n.sb += pairs

            def add_linear(blocks, gated=False):
                for lo, width in blocks:
                    for t in range(NT):
                        v.wait_ge(proj_done, 2 * n.load + 1 + t)
                        piece = hid[:, t, lo:lo + width]
                        if gated:
                            V.tensor_tensor(tok[:, t, lo:lo + width], proj_ps[t][:, 0:width],
                                            modrow[:, 1, lo:lo + width], ALU.mult).then_inc(ln_ev, 1)
                            v.drain()
                            V.tensor_tensor(piece, piece, tok[:, t, lo:lo + width], ALU.add)
                        else:
                            V.tensor_tensor(piece, piece, proj_ps[t][:, 0:width], ALU.add).then_inc(ln_ev, 1)
                    n.load += 1
                    n.lin += 1
                v.drain()
                v.sem_inc(hid_ready, 1)
                n.hidden += 1

            def out_proj(kc):
                copy_even(kc)
                add_linear(WO_BLOCKS)

            def mla():
                n.load += len(MLA_BLOCKS)
                n.lin += len(MLA_BLOCKS)
                n.rstd += 1
                v.wait_ge(rstd_ready, n.rstd)
                for t in range(NT):
                    V.tensor_scalar(tok[:, t, 0:MLA_Q_RANK], mla_c[:, t, 0:MLA_Q_RANK], rstd[:, t:t + 1], None,
                                    ALU.mult)
                    V.tensor_scalar(tok[:, t, MLA_Q_RANK:MLA_Q_RANK + MLA_KV_RANK],
                                    mla_c[:, t, MLA_Q_RANK:MLA_Q_RANK + MLA_KV_RANK], rstd[:, 2 + t:3 + t], None,
                                    ALU.mult).then_inc(nm_scaled, 1)
                kr = mla_c[:, :, MLA_IN - MLA_ROPE:MLA_IN].unsqueeze(2)
                half = MLA_ROPE // 2
                y = kr_sb[:, :, :].unsqueeze(2)
                rotate(kr[:, :, :, 0:half], kr[:, :, :, half:], y[:, :, :, 0:half], y[:, :, :, half:], 1,
                       ROT_DIM // 2, half)
                v.drain()
                copy_even(5, lambda c: mla_gains[:, c:c + 1])
                attend("mla")
                out_proj(KC)

            def final_norm():
                norm()
                v.drain()
                V.tensor_tensor(hid[:], tok[:], grow[:, :].unsqueeze(1).broadcast_to([P, NT, D]),
                                ALU.mult).then_inc(hid_ready, 1)
                n.hidden += 1

            def modulation(l):
                V.tensor_copy(condT[:], cond[:, :].unsqueeze(2).broadcast_to([P, KC, P])).then_inc(condT_ready, 1)
                n.small += SMALL_DMAS * DMA
                v.wait_ge(small_in, n.small)
                for b, (first, width) in enumerate(MOD_BLOCKS):
                    for half in range(2):
                        v.wait_ge(proj_done, 2 * n.load + 1 + half)
                        lo = first + half * 256
                        k, off = lo // D, lo % D
                        src = proj_ps[half][:, 0:256]
                        if k % 3 == 2:
                            piece = modrow[:, k // 3, off:off + 256]
                            V.tensor_tensor(piece, piece, src, ALU.add).then_inc(ln_ev, 1)
                        else:
                            g = gate[:, half, 0:256].rearrange("p (a b) -> p a b", a=2)
                            V.tensor_tensor(g, src.rearrange("p (a b) -> p a b", a=2),
                                            ident[:, :].unsqueeze(1).broadcast_to([P, 2, P]), ALU.mult)\
                                .then_inc(ln_ev, 1)
                            v.drain()
                            V.tensor_reduce(modcol[:, lo // P:lo // P + 2], g, AX.X, ALU.add)
                    n.load += 1
                    n.lin += 1
                v.drain()
                cols = modcol[:, :].rearrange("p (a b) -> p a b", a=3)
                bias = vec[:, 3 + l, 0:MOD_ROWS].rearrange("p (a b) -> p a b", a=3)
                V.tensor_tensor(cols[:, :, 0:2 * KC], cols[:, :, 0:2 * KC], bias[:, :, 0:2 * KC], ALU.add)
                V.tensor_scalar(modrow[:, 0, :], modrow[:, 0, :], 0.5, None, ALU.mult)
                V.tensor_scalar(modrow[:, 2, :], modrow[:, 2, :], 0.5, None, ALU.mult)
                mu, ka, sub = VEC_2["mu"], VEC_2["k_a"], VEC_2["subln"]
                V.tensor_scalar(one_less[:, 0:15], vec[:, 1 + l, mu:mu + 15], -1.0, 1.0, ALU.mult, ALU.add)
                V.tensor_scalar(one_less[:, 15:19], vec[:, 1 + l, ka:ka + BC], -1.0, 1.0, ALU.mult, ALU.add)
                V.tensor_scalar(vec[:, 1 + l, sub:sub + 1], vec[:, 1 + l, sub:sub + 1], 1.0 - lam_init(l), None,
                                ALU.mult)
                v.drain()
                w = vec[:, 1 + l, VEC_2["norm_w"]:VEC_2["norm_w"] + 3 * KC].rearrange("p (a b) -> p a b", a=3)
                V.scalar_tensor_tensor(modA[:], cols[:, :, KC:2 * KC], 1.0, w, ALU.add, ALU.mult)
                v.drain()

            def modulated(k):
                return lambda c: modA[:, k, c:c + 1], lambda c: modcol[:, 3 * k * KC + c:3 * k * KC + c + 1]

            def rwkv(l):
                def scalars(name, c):
                    at = VEC_2[name] + c
                    return vec[:, 1 + l, at:at + 1]

                for b, (lo, width) in enumerate(RWKV_BLOCKS):
                    for half in range(2):
                        n.shift += 1
                        v.wait_ge(shift_part, n.shift)
                        for q, dst in shift_places(b, half):
                            m = min(P, width - (2 * half + q) * P)
                            mu = scalars("mu", 4 * b + 2 * half + q)
                            last = V.scalar_tensor_tensor(dst[0:m, 1:SEQ], proj_ps[half][0:m, q * SEQ:(q + 1) * SEQ - 1],
                                                          mu[0:m], dst[0:m, 1:SEQ], ALU.mult, ALU.add)
                        last.then_inc(ln_ev, 1)
                    n.load += 1
                    n.lin += 1
                v.drain()
                flat = "p c s -> p (c s)"
                for c in range(BC):
                    V.tensor_scalar(rw_kk[:, c], rw_k[:, c], scalars("k_k", c), None, ALU.mult)
                v.drain()
                V.tensor_tensor(rw_t0, rw_kk, rw_kk, ALU.mult).then_inc(*rw_v.next("kk_sq"))
                v.wait_ge(*rw_act.at(l, "kk_norm"))
                V.tensor_scalar(rw_t2, rw_t2, 1e-12, None, ALU.max)
                v.drain()
                V.reciprocal(rw_t2, rw_t2)
                v.drain()
                V.tensor_tensor(rw_kk, rw_kk, rw_t2, ALU.mult)
                v.drain()
                for c in range(BC):
                    V.tensor_scalar(rw_t2[:, c], rw_a[:, c], scalars("k_a", c), one_less[:, 15 + c:16 + c],
                                    ALU.mult, ALU.add)
                v.drain()
                V.tensor_tensor(rw_k, rw_k, rw_t2, ALU.mult)
                V.tensor_tensor(rw_a, rw_a, rw_kk, ALU.mult)
                v.drain()
                for c in range(BC):
                    last = V.scalar_tensor_tensor(rw_t0[:, c], rw_r[:, c], scalars("r_k", c), rw_k[:, c],
                                                  ALU.mult, ALU.mult)
                last.then_inc(*rw_v.next("rk"))
                V.tensor_scalar(rw_t1, rw_t1, -math.exp(-0.5), None, ALU.mult)
                v.drain()
                for c in range(BC):
                    V.tensor_tensor_scan(rw_p[:, c], restart[:, :], rw_t1[:, c], 0.0, ALU.mult, ALU.add)
                v.drain()
                V.tensor_tensor(kr_all[:, :, 0], rw_p, rw_t1, ALU.subtract)
                p_blk = rw_p.rearrange(flat).rearrange("p (g h j) -> p g h j", h=2, j=BLK)
                k1_blk = k1.rearrange(flat).rearrange("p (g h j) -> p g h j", h=2, j=BLK)
                total = p_blk[:, :, :, BLK - 1:BLK].broadcast_to([P, 2 * BC, 2, BLK])
                V.tensor_tensor(k1_blk[:, :, 0], total[:, :, 0], p_blk[:, :, 0], ALU.subtract)
                V.tensor_scalar(k1_blk[:, :, 1], p_blk[:, :, 1], -1.0, None, ALU.mult)
                V.tensor_tensor(k_end[:, :, BLK:P], rw_p[:, :, P - 1:P].broadcast_to([P, BC, BLK]),
                                rw_p[:, :, BLK:P], ALU.subtract)
                v.drain()
                V.tensor_tensor(k_end[:, :, 0:BLK], k1[:, :, 0:BLK], rw_p[:, :, P - 1:P].broadcast_to([P, BC, BLK]),
                                ALU.add)
                first = rw_p[:, :, P + BLK - 1:P + BLK].broadcast_to([P, BC, BLK])
                V.tensor_copy(kr_in[:, :, 0, 0:BLK], kr_all[:, :, 0, P:P + BLK])
                V.tensor_copy(kr_in[:, :, 1, 0:BLK], rw_p[:, :, P:P + BLK])
                V.tensor_tensor(kr_in[:, :, 0, BLK:P], kr_all[:, :, 0, P + BLK:SEQ], first, ALU.add)
                V.tensor_tensor(kr_in[:, :, 1, BLK:P], rw_p[:, :, P + BLK:SEQ], first, ALU.add)\
                    .then_inc(*rw_v.next("expo"))
                v.wait_ge(*rw_pe.at(l, "bonus"))
                for half in range(2):
                    V.tensor_tensor(gate[:, half, :], proj_ps[half][:, :],
                                    rw_v_[:, 2 * half:2 * half + 2].rearrange(flat), ALU.mult)
                v.wait_ge(*rw_act.at(l, "exps"))
                V.tensor_tensor(kr_all[:, :, 0], kr_all[:, :, 0], rw_kk, ALU.mult)
                V.tensor_tensor(kr_all[:, :, 1], kr_all[:, :, 1], rw_r, ALU.mult)
                V.tensor_tensor(kr_in[:, :, 0], kr_in[:, :, 0], rw_kk[:, :, P:SEQ], ALU.mult)
                V.tensor_tensor(kr_in[:, :, 1], kr_in[:, :, 1], rw_r[:, :, P:SEQ], ALU.mult)
                V.tensor_tensor(bh, kh, rw_a, ALU.mult)
                V.tensor_tensor(b1, k1, rw_a, ALU.mult)
                V.tensor_tensor(b_end, k_end, rw_a[:, :, 0:P], ALU.mult)
                v.drain()
                V.tensor_tensor(kh, kh, rw_k, ALU.mult)
                V.tensor_tensor(k1, k1, rw_k, ALU.mult)
                V.tensor_tensor(k_end, k_end, rw_k[:, :, 0:P], ALU.mult)
                v.drain()
                v.sem_inc(*rw_v.next("scaled"))
                q_n = "p q n -> p (q n)"
                for t in range(NT):
                    if t == 1:
                        v.wait_ge(*rw_pe.at(l, "state"))
                        V.tensor_tensor(state, down_ps[0][:, :].rearrange("p (c n) -> p c n", n=P),
                                        headsum[:, :].unsqueeze(1).broadcast_to([P, BC, P]), ALU.mult)\
                            .then_inc(*rw_v.next("state_c"))
                    for q in range(8):
                        v.wait_ge(*rw_pe.at(l, f"mat{t}", q))
                        V.tensor_tensor(mats[:, q].rearrange(q_n), down_ps[q % 4][:, :],
                                        prod_mask[:].rearrange("p a b n -> p (a b n)"), ALU.mult)\
                            .then_inc(*rw_v.next(f"mats{t}"))
                    v.drain()
                    V.tensor_tensor(invT, mats[:, :, 2, :], lvl[:, 0, :].unsqueeze(1).broadcast_to([P, 8, P]),
                                    ALU.mult)
                    v.drain()
                    V.tensor_tensor(invT, ident[:, :].unsqueeze(1).broadcast_to([P, 8, P]), invT,
                                    ALU.subtract).then_inc(*rw_v.next(f"xt{t}"))
                    v.wait_ge(*rw_pe.at(l, f"x0{t}"))
                    for half, ps in enumerate((turn_ps, aux_ps)):
                        last = V.tensor_copy(inv[:, 4 * half:4 * half + 4].rearrange(q_n), ps[:, :])
                    last.then_inc(*rw_v.next(f"x{t}"))
                    for i in range(LV):
                        v.wait_ge(*rw_pe.at(l, f"yz{t}_{i}", 1))
                        for half in range(2):
                            rows = slice(4 * half, 4 * half + 4)
                            if i < LV - 1:
                                x = inv[:, rows].rearrange(q_n)
                                V.tensor_tensor(x, x, down_ps[half][:, :], ALU.subtract)
                            x = invT[:, rows].rearrange(q_n)
                            last = V.tensor_tensor(x, x, down_ps[2 + half][:, :], ALU.subtract)
                        last.then_inc(*rw_v.next(f"x{t}"))
                    v.wait_ge(*rw_pe.at(l, f"u{t}"))
                    V.tensor_scalar(u_neg, aux_ps[:, :], -1.0, None, ALU.mult).then_inc(*rw_v.next(f"un{t}"))
                v.wait_ge(*rw_act.at(l, "oc1"))
                o, sq = (tok[:, :, k * W_B:(k + 1) * W_B].rearrange("p t (h d) -> p t h d", d=N_B) for k in range(2))
                stats = [x.rearrange("p (t h) -> p t h", t=NT) for x in (ln_ss[:, :], ln_rs[:, :])]
                V.tensor_reduce(stats[0], o, AX.X, ALU.add)
                v.drain()
                V.tensor_scalar(ln_ss[:, :], ln_ss[:, :], 1.0 / N_B, None, ALU.mult)
                v.drain()
                V.tensor_tensor(o, o, stats[0].unsqueeze(3).broadcast_to([P, NT, H_B, N_B]), ALU.subtract)
                v.drain()
                V.tensor_tensor(sq, o, o, ALU.mult)
                v.drain()
                V.tensor_reduce(stats[0], sq, AX.X, ALU.add).then_inc(*rw_v.next("ln_ss"))
                v.wait_ge(*rw_pool.at(l, "ln_rs"))
                V.tensor_tensor(o, o, stats[1].unsqueeze(3).broadcast_to([P, NT, H_B, N_B]), ALU.mult)\
                    .then_inc(*rw_v.next("ln"))
                copy_even(BC, lambda c: scalars("ln_w", c), lambda c: scalars("ln_b", c), oT[1])
                v.wait_ge(ev_odd, n.odd)
                v.drain()
                V.tensor_tensor(oT[1][:], oT[1][:], gate[:].rearrange("p t n -> p (t n)")
                                .rearrange("p (c s) -> p c s", c=BC), ALU.add)
                v.drain()
                V.tensor_tensor(oT[1][:], oT[1][:], oT[2][:], ALU.mult).then_inc(*rw_v.next("out"))

            def hgrn(l):
                n.load += 4
                n.lin += 4
                v.wait_ge(ln_ev, 2 * (n.lin - 2))
                V.tensor_scalar(h_t, hf, -1.0, None, ALU.mult)
                v.drain()
                V.tensor_tensor(h_t, h_t, hf, ALU.max).then_inc(*hg_abs.next("abs"))
                V.memset(hs, 0.0)
                v.wait_ge(*hg_ln.at(l, "ln"))
                V.scalar_tensor_tensor(hf, hf, 0.0, h_t, ALU.min, ALU.subtract)
                if l > 0:
                    v.drain()
                    for c in range(BC):
                        V.tensor_scalar(hf[:, c], hf[:, c], lows[:, 4, c:c + 1], None, ALU.add)
                        V.tensor_scalar(hk[:, c], hk[:, c], lows[:, 2, c:c + 1], None, ALU.mult)
                    v.drain()
                    V.tensor_scalar(h_t, hf, -1.0, None, ALU.mult)
                    v.drain()
                    V.tensor_tensor(h_t, h_t, hf, ALU.max).then_inc(*hb_abs.next("abs"))
                    v.wait_ge(*hb_ln.at(0, "ln"))
                    V.scalar_tensor_tensor(hf, hf, 0.0, h_t, ALU.max, ALU.add)
                    v.drain()
                    for c in range(BC):
                        V.tensor_scalar(hf[:, c], hf[:, c], lows[:, 0, c:c + 1], None, ALU.add)
                v.drain()
                v.sem_inc(*hg_upd.next("upd"))

                def take(i):
                    v.wait_ge(*hg_s.at(l, "s", i))
                    banks = down_ps[0:2] if i % 2 == 0 else down_ps[2:4]
                    if i == n_lv:
                        last = V.tensor_copy(h_cross.rearrange("p c n -> p (c n)"), banks[0][:, :])
                    else:
                        m = ident[:, :] if i == 0 else lvl[:, i - 1, :]
                        v.drain()
                        for half in range(2):
                            dst = (h_acc if i == 0 else h_t.rearrange("p c s -> p (c s)")
                                   .rearrange("p (q n) -> p q n", n=P))[:, 4 * half:4 * half + 4]
                            last = V.tensor_tensor(dst, banks[half][:, :].rearrange("p (q n) -> p q n", n=P),
                                                   m.unsqueeze(1).broadcast_to([P, 4, P]), ALU.mult)
                        if i:
                            v.drain()
                            last = V.tensor_tensor(h_acc, h_acc, h_t.rearrange("p c s -> p (c s)")
                                                   .rearrange("p (q n) -> p q n", n=P), ALU.add)
                    last.then_inc(*hg_acc.next("acc"))

                for i, m in enumerate(LEVELS + [P]):
                    v.wait_ge(*hg_ex.at(l, "ex", i))
                    if i >= 2:
                        v.wait_ge(*hg_s.at(l, "s", i - 1))
                    e, x, q, k = (halves(y, m) for y in (h_e, h_x[i % 2], hq, hk))
                    V.tensor_tensor(x[:, :, 1], e[:, :, 1], q[:, :, 1], ALU.mult)
                    V.tensor_tensor(x[:, :, 0], e[:, :, 0], k[:, :, 0], ALU.mult).then_inc(*hg_x.next("x"))
                    if i < len(LEVELS):
                        f, g = halves(hf, m), halves(hs, m)
                        shape = [P, BC * SEQ // (2 * m), m]
                        V.tensor_tensor(g[:, :, 0], g[:, :, 0], f[:, :, 1, m - 1:m].broadcast_to(shape), ALU.add)
                        v.drain()
                        V.tensor_tensor(f[:, :, 1], f[:, :, 1], f[:, :, 0, m - 1:m].broadcast_to(shape),
                                        ALU.add).then_inc(*hg_upd.next("upd"))
                    take(i)
                take(n_lv)
                v.wait_ge(*hg_oc.at(l, "oc"))
                o, sq = (tok[:, :, k * W_C:(k + 1) * W_C].rearrange("p t (h d) -> p t h d", d=DK_C) for k in range(2))
                V.tensor_tensor(sq, o, o, ALU.mult)
                v.drain()
                V.tensor_reduce(ln_ss[:, 0:8].rearrange("p (t h) -> p t h", t=NT), sq, AX.X, ALU.add)\
                    .then_inc(*hg_ss.next("ss"))
                V.tensor_tensor(o, o, h_g.rearrange("p t (h d) -> p t h d", d=DK_C), ALU.mult)
                v.drain()
                v.wait_ge(*hg_rs.at(l, "rs"))
                V.tensor_tensor(o, o, ln_rs[:, 0:8].rearrange("p (t h) -> p t h", t=NT).unsqueeze(3)
                                .broadcast_to([P, NT, H_C, DK_C]), ALU.mult).then_inc(*hg_out.next("out"))
                copy_even(BC, lambda c: vec[:, 1 + l, VEC_2["hnorm"]:VEC_2["hnorm"] + 1], None, oT[2])

            def hybrid(l):
                attend("diff", l)
                copy_even(BC, lambda c: vec[:, 1 + l, VEC_2["subln"]:VEC_2["subln"] + 1], None, oT[0])
                rwkv(l)
                hgrn(l)
                for i in range(3):
                    for lo, width in WO_BLOCKS:
                        n.load += 1
                        n.lin += 1
                        for t in range(NT):
                            if t == 0:
                                v.wait_ge(ln_ev, 2 * n.lin)
                            v.wait_ge(proj_done, 2 * n.load + 1 + t)
                            sum_at = tok[:, t, lo:lo + width]
                            if i == 0:
                                V.tensor_tensor(sum_at, proj_ps[t][:, :], gate[:, t, :], ALU.mult).then_inc(ln_ev, 1)
                            else:
                                V.tensor_tensor(gate[:, t, :], proj_ps[t][:, :], gate[:, t, :], ALU.mult)
                                v.drain()
                                V.tensor_tensor(sum_at, sum_at, gate[:, t, :], ALU.add).then_inc(ln_ev, 1)
                        n.load += 1
                        n.lin += 1
                v.drain()
                v.sem_inc(y_ready, 1)
                copy_even(KC)
                add_linear(WO_BLOCKS, gated=True)

            v.wait_ge(const_in, CONST_DMAS * DMA)
            v.wait_ge(masks_ready, 1)
            V.tensor_copy(pos[:, 1, :], pos_i[:, :])
            v.drain()
            v.wait_ge(vec_turned, 1)
            for i, rows in enumerate(VEC_ROWS):
                last = V.tensor_copy(vec[:, i, 0:rows], turn_ps[:, i * P:i * P + rows] if i < 4 else aux_ps[:, 0:rows])
            last.then_inc(vec_ready, 1)
            v.drain()
            V.tensor_copy(pos[:, 0, :], vec[:, 0, VEC_1["index"]:VEC_1["index"] + NT])
            V.tensor_tensor(lqk[:, :, 0], lqk[:, :, 0], lqk[:, :, 1], ALU.mult)
            V.tensor_tensor(lqk[:, :, 2], lqk[:, :, 2], lqk[:, :, 3], ALU.mult)
            b0, b1_ = VEC_2["bound0"], VEC_2["bound1"]
            V.tensor_tensor(lows[:, 5], vec[:, 2, b0:b0 + BC], vec[:, 2, b1_:b1_ + BC], ALU.subtract)
            v.drain()
            for k in range(2):
                last = V.tensor_reduce(lam_e[:, :, k], lqk[:, :, 2 * k], AX.X, ALU.add)
            last.then_inc(lam_terms, 1)
            V.tensor_scalar(lows[:, 0], lows[:, 5], -1.0, None, ALU.mult)
            v.drain()
            V.tensor_tensor(lows[:, 3], lows[:, 0], lows[:, 5], ALU.max).then_inc(low_d, 1)
            split = NROPE - DH // 2
            for stack, (a, b) in enumerate(((0, split), (split, NROPE))):
                for t in range(NT):
                    V.tensor_scalar(ang[:, 1, t, a:b], freq[:, a:b], pos[:, stack, t:t + 1], None, ALU.mult)
            v.drain()
            V.tensor_scalar(angk[:, 1], ang[:, 1], 1.0 / (2 * math.pi), None, ALU.mult)
            v.drain()
            V.tensor_scalar(angk[:, 1], angk[:, 1], ROUND, None, ALU.add)
            v.drain()
            V.tensor_scalar(angk[:, 1], angk[:, 1], ROUND, None, ALU.subtract)
            for part in TWO_PI:
                v.drain()
                V.scalar_tensor_tensor(ang[:, 1], angk[:, 1], -part, ang[:, 1], ALU.mult, ALU.add)
            v.drain()
            V.tensor_scalar(ang[:, 0], ang[:, 1], math.pi / 2, None, ALU.add)
            v.drain()
            V.tensor_scalar(angk[:, 0], ang[:, 0], math.pi, -2 * math.pi, ALU.is_gt, ALU.mult)
            v.drain()
            V.tensor_tensor(ang[:, 0], ang[:, 0], angk[:, 0], ALU.add)
            v.drain()
            V.tensor_scalar(ang[:], ang[:], PI_DOWN, -PI_DOWN, ALU.min, ALU.max).then_inc(trig_ang, 1)
            v.wait_ge(lam_exp, 1)
            V.tensor_tensor(lam[:, :], lam_e[:, :, 0], lam_e[:, :, 1], ALU.subtract)
            v.wait_ge(low_s, 1)
            V.scalar_tensor_tensor(lows[:, 1], lows[:, 0], 0.0, lows[:, 3], ALU.max, ALU.add)
            v.drain()
            V.scalar_tensor_tensor(lows[:, 0], lows[:, 5], 0.0, lows[:, 3], ALU.max, ALU.add)
            v.drain()
            for l in range(DEPTH_2):
                V.tensor_scalar(lam[:, l:l + 1], lam[:, l:l + 1], lam_init(l), None, ALU.add)
            V.tensor_tensor(lows[:, 4], lows[:, 0], lows[:, 1], ALU.subtract)
            v.drain()
            V.tensor_scalar(lows[:, 0:2], lows[:, 0:2], -1.0, None, ALU.mult).then_inc(low_d, 1)
            v.wait_ge(low_s, 2)
            v.wait_ge(trig_ready, 1)
            v.wait_ge(cond_ready, 1)

            def gained(k):
                return lambda c: gains[:, k, c:c + 1]

            for l in range(DEPTH):
                ffn(gained(3 * l))
                norm()
                copy_even(KC, gained(3 * l + 1))
                if l % 3 == 2:
                    mla()
                else:
                    attend("sb" if l % 3 == 0 else "moba")
                    out_proj(KC)
                ffn(gained(3 * l + 2))
            final_norm()
            for l in range(DEPTH_2):
                modulation(l)
                ffn(*modulated(0), row=0)
                norm()
                copy_even(KC, *modulated(1))
                hybrid(l)
                ffn(*modulated(2), row=2)


def lam_init(layer):
    return 0.8 - 0.6 * math.exp(-0.3 * layer)


ARENA = 20224
CONSTANTS_END = 11712
WO_BLOCKS = [(0, 512), (512, 512)]
MOD_BLOCKS = [(i * 512, 512) for i in range(N_MOD * D // 512)]
RWKV_BLOCKS = [(P_A, 512), (P_A + 512, 512), (P_A + 1024, 512), (P_A + 1536, P_B - 1536)]
HGRN_BLOCKS = [(P_A + P_B + i * 512, 512) for i in range(4)]
MLA_BLOCKS = [(0, 512), (512, MLA_IN - 512)]
CONST_DMAS = 5
VEC_DMAS = 3 * DEPTH + 4 + DEPTH_2 * 15
SMALL_DMAS = 7
ROUND = 1.5 * 2.0 ** 23
PI_DOWN = float(np.nextafter(np.float32(math.pi), np.float32(0)))


def _two_pi_parts():
    parts, rest = [], 2 * math.pi
    for e in (8, 19, 30):
        part = math.floor(rest * 2.0 ** e) / 2.0 ** e
        parts.append(part)
        rest -= part
    return parts


TWO_PI = _two_pi_parts()


_INS = ["x", "norm_ffn1", "ffn1_w_gate_up", "ffn1_w_down", "norm_mix", "norm_ffn2", "ffn2_w_gate_up", "ffn2_w_down",
        "sb_w_qkv", "sb_w_o", "moba_w_qkv", "moba_w_o", "mla_w_in", "mla_q_norm", "mla_w_uq", "mla_kv_norm",
        "mla_w_ukv", "mla_w_o", "final_norm", "c_2", "positions_2", "mod_w_2", "mod_b_2", "norm_w_2",
        "ffn_w_gate_2", "ffn_w_up_2", "ffn_w_down_2", "w_in_2", "qk_norm_w_2", "lambda_qk_2", "subln_w_2",
        "w_out_a_2", "rwkv_mu_2", "rwkv_w0_2", "rwkv_w2_2", "rwkv_a0_2", "rwkv_a2_2", "rwkv_g2_2", "rwkv_k_k_2",
        "rwkv_k_a_2", "rwkv_r_k_2", "rwkv_ln_w_2", "rwkv_ln_b_2", "w_out_b_2", "hgrn_lower_bounds_2",
        "hgrn_norm_w_2", "w_out_c_2", "w_out_2"]


def shape_constants():
    def frequencies(theta, width):
        return np.float32(theta) ** (-np.arange(0, width, 2, dtype=np.float32) / np.float32(width))
    return {"rope_freq": np.concatenate([frequencies(ROPE_THETA, ROT_DIM), frequencies(ROPE_THETA, MLA_ROPE),
                                         frequencies(ROPE_THETA_2, DH_A)]).astype(np.float32),
            "token_index": np.arange(SEQ, dtype=np.float32)}


def kernel(**inputs):
    import concourse.bacc as _bacc
    from concourse.bass_utils import run_bass_kernel_spmd as _run

    nc = _bacc.Bacc("TRN2", target_bir_lowering=False, num_devices=1)
    sources = {name: inputs[name] for name in _INS}
    sources.update(shape_constants())
    arrays, aps = {}, {}
    for name, source in sources.items():
        a = np.ascontiguousarray(source)
        arrays[f"in_{name}"] = a
        aps[name] = nc.dram_tensor(f"in_{name}", a.shape, mybir.dt.from_np(a.dtype), kind="ExternalInput").ap()
    out = nc.dram_tensor("out_0", (1, SEQ, D), F32, kind="ExternalOutput").ap()
    program(nc, aps, out)
    result = _run(nc, [arrays], core_ids=[0])
    return result.results[0]["out_0"]
```
